# Optimizing a Trainium2 kernel written in Bass

```python
import math
import jax, jax.numpy as jnp
from jax import lax
import numpy as np

D_MODEL = 1024
BATCH = 1
SEQ = 512
DEPTH = 2

CHUNK = 64
N_HEADS_DN = 8
HEAD_DIM_DN = 128
KEY_WIDTH = N_HEADS_DN * HEAD_DIM_DN
SHORT_CONV = 4
CONV_CH = D_MODEL
DW_WIDTH = 31
D_FF = 2816
IN_COLS = 4 * KEY_WIDTH + 2 * N_HEADS_DN + 2 * CONV_CH + 2 * D_MODEL
EPS = 1e-6

kernel_name = 'hybrid_gdn_conformer_macaron_trunk'

def rmsnorm(x, w):
    xf = x.astype(jnp.float32)
    y = xf * lax.rsqrt(jnp.mean(xf * xf, axis=-1, keepdims=True) + EPS)
    return (y * w.astype(jnp.float32)).astype(x.dtype)

def l2norm(x):
    xf = x.astype(jnp.float32)
    return xf * lax.rsqrt(jnp.sum(xf * xf, axis=-1, keepdims=True) + EPS)

def swiglu(x, w_gate, w_up, w_down):
    return (jax.nn.silu(x @ w_gate) * (x @ w_up)) @ w_down

def causal_depthwise_conv(x, w):
    width = w.shape[0]
    return lax.conv_general_dilated(
        x, w[:, None, :].astype(x.dtype), window_strides=(1,),
        padding=[(width - 1, 0)], dimension_numbers=('NWC', 'WIO', 'NWC'),
        feature_group_count=x.shape[-1])

def gated_delta_chunked(q, k, v, g, beta):
    bsz, seq, heads, dk = q.shape
    dv = v.shape[-1]
    n_chunks = seq // CHUNK

    def to_chunks(t):
        return t.reshape(bsz, n_chunks, CHUNK, heads, -1).transpose(0, 3, 1, 2, 4)

    q, k, v = to_chunks(q), to_chunks(k), to_chunks(v)
    g = g.reshape(bsz, n_chunks, CHUNK, heads).transpose(0, 3, 1, 2)
    beta = beta.reshape(bsz, n_chunks, CHUNK, heads).transpose(0, 3, 1, 2)
    gc = jnp.cumsum(g, axis=-1)
    idx = jnp.arange(CHUNK)
    strict = idx[:, None] > idx[None, :]
    incl = idx[:, None] >= idx[None, :]
    diff = gc[..., :, None] - gc[..., None, :]
    decay_strict = jnp.exp(jnp.where(strict, diff, -jnp.inf))
    decay_incl = jnp.exp(jnp.where(incl, diff, -jnp.inf))

    kb = k * beta[..., None]
    m = jnp.einsum('bhnid,bhnjd->bhnij', kb, k) * decay_strict
    eye = jnp.eye(CHUNK, dtype=m.dtype)
    rhs = jnp.concatenate([v * beta[..., None], kb * jnp.exp(gc)[..., None]], axis=-1)
    sol = lax.linalg.triangular_solve(eye + m, rhs, left_side=True, lower=True)
    u, w = sol[..., :dv], sol[..., dv:]

    attn = jnp.einsum('bhnid,bhnjd->bhnij', q, k) * decay_incl
    g_last = gc[..., -1]
    qd = q * jnp.exp(gc)[..., None]
    kd = k * jnp.exp(g_last[..., None] - gc)[..., None]
    xs = tuple(jnp.moveaxis(t, 2, 0) for t in (u, w, qd, kd, attn, jnp.exp(g_last)))

    def step(state, inp):
        u_c, w_c, qd_c, kd_c, a_c, eg = inp
        v_new = u_c - jnp.einsum('bhck,bhkv->bhcv', w_c, state)
        o = jnp.einsum('bhck,bhkv->bhcv', qd_c, state) + jnp.einsum('bhij,bhjv->bhiv', a_c, v_new)
        state = state * eg[..., None, None] + jnp.einsum('bhck,bhcv->bhkv', kd_c, v_new)
        return state, o

    s0 = jnp.zeros((bsz, heads, dk, dv), jnp.float32)
    _, o = lax.scan(step, s0, xs)
    return o.transpose(1, 0, 3, 2, 4).reshape(bsz, seq, heads, dv)

def hybrid_mixer(h, w_in, qkv_conv_w, a_log, dt_bias, head_norm, w_a_out,
                 dw_conv_w, dw_conv_b, conv_norm, w_b_out, w_o):
    bsz, seq, _ = h.shape
    proj = h @ w_in
    bounds = np.cumsum([3 * KEY_WIDTH, KEY_WIDTH, N_HEADS_DN, N_HEADS_DN, 2 * CONV_CH]).tolist()
    qkv, g_out, a, b, glu, gates = jnp.split(proj, bounds, axis=-1)

    qkv = jax.nn.silu(causal_depthwise_conv(qkv, qkv_conv_w))
    q, k, v = jnp.split(qkv, 3, axis=-1)
    shp = (bsz, seq, N_HEADS_DN, HEAD_DIM_DN)
    q = l2norm(q.reshape(shp)) * (HEAD_DIM_DN ** -0.5)
    k = l2norm(k.reshape(shp))
    v = v.reshape(shp).astype(jnp.float32)
    beta = jax.nn.sigmoid(b.astype(jnp.float32))
    g = -jnp.exp(a_log.astype(jnp.float32)) * jax.nn.softplus(
        a.astype(jnp.float32) + dt_bias.astype(jnp.float32))
    o = gated_delta_chunked(q, k, v, g, beta)
    o = rmsnorm(o, head_norm) * jax.nn.silu(g_out.reshape(shp).astype(jnp.float32))
    y_a = o.reshape(bsz, seq, KEY_WIDTH).astype(h.dtype) @ w_a_out

    val, gt = jnp.split(glu, 2, axis=-1)
    c = val * jax.nn.sigmoid(gt)
    c = causal_depthwise_conv(c, dw_conv_w) + dw_conv_b
    c = jax.nn.silu(rmsnorm(c, conv_norm))
    y_b = c @ w_b_out

    gate_a, gate_b = jnp.split(gates, 2, axis=-1)
    merged = jax.nn.sigmoid(gate_a) * y_a + jax.nn.sigmoid(gate_b) * y_b
    return merged @ w_o

def setup_inputs(seed: int = 0) -> dict:
    key = jax.random.key(seed)
    ks = jax.random.split(key, 24)

    def nrm(k, shape, scale):
        return jax.random.normal(k, shape, jnp.float32) * scale

    def gain(k, shape):
        return 1.0 + 0.02 * jax.random.normal(k, shape, jnp.float32)

    dt = jnp.exp(jax.random.uniform(ks[9], (DEPTH, N_HEADS_DN), jnp.float32,
                                    minval=float(np.log(1e-3)), maxval=float(np.log(1e-1))))
    return {
        'x': nrm(ks[0], (BATCH, SEQ, D_MODEL), 1.0),
        'ffn1_norm': gain(ks[1], (DEPTH, D_MODEL)),
        'ffn1_w_gate': nrm(ks[2], (DEPTH, D_MODEL, D_FF), D_MODEL ** -0.5),
        'ffn1_w_up': nrm(ks[3], (DEPTH, D_MODEL, D_FF), D_MODEL ** -0.5),
        'ffn1_w_down': nrm(ks[4], (DEPTH, D_FF, D_MODEL), D_FF ** -0.5),
        'mix_norm': gain(ks[5], (DEPTH, D_MODEL)),
        'w_in': nrm(ks[6], (DEPTH, D_MODEL, IN_COLS), D_MODEL ** -0.5),
        'qkv_conv_w': nrm(ks[7], (DEPTH, SHORT_CONV, 3 * KEY_WIDTH), SHORT_CONV ** -0.5),
        'a_log': jnp.log(jax.random.uniform(ks[8], (DEPTH, N_HEADS_DN), jnp.float32,
                                            minval=1.0, maxval=16.0)),
        'dt_bias': dt + jnp.log(-jnp.expm1(-dt)),
        'head_norm': gain(ks[10], (DEPTH, HEAD_DIM_DN)),
        'w_a_out': nrm(ks[11], (DEPTH, KEY_WIDTH, D_MODEL), KEY_WIDTH ** -0.5),
        'dw_conv_w': nrm(ks[12], (DEPTH, DW_WIDTH, CONV_CH), DW_WIDTH ** -0.5),
        'dw_conv_b': nrm(ks[13], (DEPTH, CONV_CH), 0.02),
        'conv_norm': gain(ks[14], (DEPTH, CONV_CH)),
        'w_b_out': nrm(ks[15], (DEPTH, CONV_CH, D_MODEL), CONV_CH ** -0.5),
        'w_o': nrm(ks[16], (DEPTH, D_MODEL, D_MODEL), D_MODEL ** -0.5),
        'ffn2_norm': gain(ks[17], (DEPTH, D_MODEL)),
        'ffn2_w_gate': nrm(ks[18], (DEPTH, D_MODEL, D_FF), D_MODEL ** -0.5),
        'ffn2_w_up': nrm(ks[19], (DEPTH, D_MODEL, D_FF), D_MODEL ** -0.5),
        'ffn2_w_down': nrm(ks[20], (DEPTH, D_FF, D_MODEL), D_FF ** -0.5),
        'final_norm': gain(ks[21], (D_MODEL,)),
    }

def reference(x, ffn1_norm, ffn1_w_gate, ffn1_w_up, ffn1_w_down, mix_norm, w_in,
              qkv_conv_w, a_log, dt_bias, head_norm, w_a_out, dw_conv_w, dw_conv_b,
              conv_norm, w_b_out, w_o, ffn2_norm, ffn2_w_gate, ffn2_w_up, ffn2_w_down,
              final_norm):
    for l in range(DEPTH):
        x = x + 0.5 * swiglu(rmsnorm(x, ffn1_norm[l]), ffn1_w_gate[l], ffn1_w_up[l], ffn1_w_down[l])
        x = x + hybrid_mixer(rmsnorm(x, mix_norm[l]), w_in[l], qkv_conv_w[l], a_log[l], dt_bias[l],
                             head_norm[l], w_a_out[l], dw_conv_w[l], dw_conv_b[l], conv_norm[l],
                             w_b_out[l], w_o[l])
        x = x + 0.5 * swiglu(rmsnorm(x, ffn2_norm[l]), ffn2_w_gate[l], ffn2_w_up[l], ffn2_w_down[l])
    return rmsnorm(x, final_norm)


_drawn_inputs = setup_inputs


def setup_inputs(seed=0):
    import zlib

    import numpy as np

    out = dict(_drawn_inputs(seed))
    spreads = {}
    factors = {'ffn1_norm': 4.189,
     'mix_norm': 3.152,
     'head_norm': 24.451,
     'dw_conv_b': 11.435,
     'conv_norm': 36.358,
     'ffn2_norm': 15.62,
     'final_norm': 20.375}
    for name, (base, spread) in spreads.items():
        noise = np.random.default_rng([zlib.crc32(name.encode()), seed]).standard_normal(out[name].shape)
        drawn = base * np.exp(spread * noise) if base else spread * noise
        out[name] = __import__('jax').numpy.asarray(drawn.astype(out[name].dtype))
    for name, factor in factors.items():
        out[name] = (out[name] * factor).astype(out[name].dtype)
    return out
```

```python
from contextlib import ExitStack

import numpy as np

import concourse.bass as bass
from concourse import mybir
from concourse.alu_op_type import AluOpType as ALU

P = 128
DEPTH, SEQ, D, FF, HEADS = 2, 512, 1024, 2816, 8
KT = D // P
FT = FF // P
NC = SEQ // P
TAPS, SC = 31, 4
EPS = 1e-6
SLOTS = 4
UNIT = KT * P
DSPLIT = [(0, 8), (8, 16), (16, 22)]
F32, F32R = mybir.dt.float32, mybir.dt.float32r
ACT = mybir.ActivationFunctionType

R_F1, R_D1, R_H, R_T, R_O, R_F2, R_D2, R_LAYER = 0, 11, 17, 29, 37, 39, 50, 56
V_F1, V_D1, V_T, V_O, V_F2, V_D2, V_LAYER = 0, 11, 17, 25, 27, 38, 44
G_LAYER = 12

C_Q, C_K, C_V, C_G, C_AB, C_VAL, C_GT, C_GA, C_GB = 0, D, 2 * D, 3 * D, 4 * D, 4 * D + 16, 5 * D + 16, 6 * D + 16, 7 * D + 16

PR_DW, PR_B, PR_CN, PR_F1, PR_MIX, PR_F2, PR_QKV, PR_N = 0, 31, 32, 33, 34, 35, 36, 48

I_ID, I_INCL, I_STRICT, I_M1T, I_LV = 0, 1, 2, 3, 4
LEVELS = 6

AB_V, AB_G = 15, 13

HS_G, HS_GC, HS_NEG, HS_BETA, HS_KD, HS_GL, HS_N = 0, 1, 2, 3, 4, 5, 6


def constants():
    r, c = np.arange(P)[:, None], np.arange(P)[None, :]
    mats = [r == c, r <= c, r < c, (r % 2 == 0) & (c == r + 1)]
    for lv in range(LEVELS):
        s = 2 << lv
        mats.append(((r // s) % 2 == 1) & (c // s == r // s - 1))
    return np.ascontiguousarray(np.stack(mats, 1).astype(np.float32))


class Steps:

    def __init__(self, sem, names):
        self.sem, self.names, self.at, self.n = sem, names, {x: i + 1 for i, x in enumerate(names)}, 0
        assert len(self.at) == len(names)

    def step(self, name):
        assert self.names[self.n % len(self.names)] == name, (name, self.names[self.n % len(self.names)])
        self.n += 1
        return self.sem, 1

    def after(self, rnd, name):
        return (rnd + 1) * len(self.names) + self.at[name]


PE_STEPS = ["gr", "kt", "kk", "sk", "kq", "vt", "x2t"]
for _l in range(LEVELS - 1):
    PE_STEPS += [f"y{_l}", f"xy{_l}", f"xt{_l}"]
PE_STEPS += [f"y{LEVELS - 1}", f"xy{LEVELS - 1}", "vn0", "os0"]
for _c in range(1, NC):
    PE_STEPS += [f"p{_c}", f"vn{_c}", f"os{_c}"]
PE_STEPS += ["so", "fb"]

DVE_STEPS = ["hs", "gbc", "kT", "qT", "vT", "dmin", "skE", "rden", "bnk2", "NT", "m1", "x2T", "attnT"]
for _l in range(LEVELS):
    DVE_STEPS += [f"y{_l}", f"x{_l}"]
DVE_STEPS += ["vn0", "s0"]
for _c in range(1, NC):
    DVE_STEPS += [f"r{_c}", f"vn{_c}"] + ([f"s{_c}"] if _c < NC - 1 else [])
DVE_STEPS += ["og", "vE", "fbc", "oF", "ohi", "olo"]

ACT_STEPS = ["sgc", "thk", "thq", "thv", "ksq", "eg", "decT", "kd", "vs", "X2"]
ACT_STEPS += [f"XT{_l}" for _l in range(LEVELS - 1)] + ["qsq", "osq"]
POOL_STEPS = ["decs", "rk", "deci", "qd", "rs"]
ACT_DENSE = ["q_raw", "q_tap", "k_raw", "k_tap", "v_raw", "v_tap", "g_th", "val", "gt_th"]
DVE_DENSE = ["dcol", "q1", "q2", "q3", "k1", "k2", "k3", "v1", "v2", "v3", "sg", "craw"]


def trunk(nc, x, ffn1_norm, ffn1_w_gate, ffn1_w_up, ffn1_w_down, mix_norm, w_in, qkv_conv_w, a_log,
          dt_bias, head_norm, w_a_out, dw_conv_w, dw_conv_b, conv_norm, w_b_out, w_o, ffn2_norm,
          ffn2_w_gate, ffn2_w_up, ffn2_w_down, final_norm, consts, out):
    ds = bass.ds
    with ExitStack() as ctx:
        place = [(nc.sbuf_base + 31) // 32 * 32]

        def sb(name, shape, dt=F32):
            t = nc.alloc_sbuf_tensor_at(name, [P, *shape], dt, offset=place[0])
            place[0] += (4 * int(np.prod(shape)) + 31) // 32 * 32
            return t

        cst = sb("cst", [I_LV + LEVELS, P])
        ident = cst[:, I_ID, :]
        incl = cst[:, I_INCL, :]
        ones = sb("ones", [P])
        xT = sb("xT", [KT, SEQ])
        h_hi = sb("h_hi", [KT, SEQ], F32R)
        h_lo = sb("h_lo", [KT, SEQ], F32R)
        raw = [sb(f"raw{s}", [UNIT]) for s in range(SLOTS)]
        w_hi = [sb(f"w_hi{s}", [UNIT], F32R) for s in range(SLOTS)]
        w_lo = [sb(f"w_lo{s}", [UNIT], F32R) for s in range(SLOTS)]
        row_at = place[0]
        prow = sb("prow", [D])
        pcol = sb("pcol", [KT, PR_N])
        ssq = sb("ssq", [SEQ])
        sqb = [sb(f"sqb{i}", [SEQ]) for i in range(2)]
        nrm = sb("nrm", [4, NC])
        pw = sb("pw", [2, NC])
        fbc = sb("fbc", [NC, P])
        hf = [sb(f"hf{i}", [SEQ]) for i in range(2)]
        hnw = sb("hnw", [1])
        hnh = sb("hnh", [1])
        hb = [*hf, *sqb]
        arena = place[0]

        act_hi = sb("act_hi", [FT, SEQ], F32R)
        act_lo = sb("act_lo", [FT, SEQ], F32R)
        sg_f, a_f = hf, sqb
        ffn_end = place[0]

        place[0] = arena
        o_hi = sb("o_hi", [HEADS, SEQ], F32R)
        o_lo = sb("o_lo", [HEADS, SEQ], F32R)
        c_at = place[0]
        c_all = sb("c_all", [KT, SEQ])
        dn_at = place[0]
        q_raw = sb("q_raw", [SEQ + SC - 1])
        k_raw = sb("k_raw", [SEQ + SC - 1])
        v_raw = sb("v_raw", [SEQ + SC - 1])
        c_raw = sb("c_raw", [SEQ + TAPS - 1])
        (qa, ka, va, cacc, qT, kT, dec, decs, attn, qd, NT, X, XT, Y) = (
            sb(n, [SEQ]) for n in "qa ka va cacc qT kT dec decs attn qd NT X XT Y".split())
        valb, gth, sgn, sgc, og = hf[0], hf[1], sqb[0], sqb[1], ssq
        S, R, VN = (sb(n, [P]) for n in ("S", "R", "VN"))
        hsc = sb("hsc", [HEADS, HS_N, NC])
        hs = sb("hs", [HS_N, NC])
        sm = sb("sm", [6, NC])
        ncol = sb("ncol", [PR_N])
        dcol = sb("dcol", [PR_N])
        dn_end = place[0]
        place[0] = c_at
        ab = sb("ab", [NC, 16])
        abT = sb("abT", [SEQ])
        abw = sb("abw", [8, HEADS, NC])
        alb = sb("alb", [2, HEADS])
        wab_raw = sb("wab_raw", [KT, 16])
        wab_hi = sb("wab_hi", [KT, 16], F32R)
        wab_lo = sb("wab_lo", [KT, 16], F32R)
        place[0] = row_at
        kd = sb("kd", [SEQ])
        vs = sb("vs", [SEQ])
        place[0] = dn_at
        c_hi = sb("c_hi", [KT, SEQ], F32R)
        c_lo = sb("c_lo", [KT, SEQ], F32R)
        cth = [sb(f"cth{i}", [SEQ]) for i in range(2)]
        assert max(place[0], ffn_end, dn_end) <= nc.sbuf_usable_end, (place[0], ffn_end, dn_end, nc.sbuf_usable_end)
        place[0] = c_at
        mg = sb("mg", [KT, SEQ])
        place[0] = arena
        mg_hi = sb("mg_hi", [KT, SEQ], F32R)
        mg_lo = sb("mg_lo", [KT, SEQ], F32R)
        thA, thB, t0, t1 = hf[0], hf[1], sqb[0], sqb[1]

        bank = [ctx.enter_context(nc.psum_tensor(f"bank{i}", [P, SEQ], F32)) for i in range(8)]

        def sem(name):
            return ctx.enter_context(nc.semaphore(name))

        const_in = sem("const_in")
        init = sem("init")
        raw_landed = [sem(f"raw_landed{s}") for s in range(SLOTS)]
        hi_done = sem("hi_done")
        lo_v = sem("lo_v")
        lo_g = sem("lo_g")
        used = sem("used")
        xt_done = sem("xt_done")
        x_upd = sem("x_upd")
        sq_done = sem("sq_done")
        ssq_done = sem("ssq_done")
        stat = sem("stat")
        var_done = sem("var_done")
        rs_done = sem("rs_done")
        fbc_done = sem("fbc_done")
        bc = sem("bc")
        hf_done = sem("hf_done")
        hhi_done = sem("hhi_done")
        hlo_g = sem("hlo_g")
        hlo_v = sem("hlo_v")
        silu_done = sem("silu_done")
        prod_done = sem("prod_done")
        acthi_done = sem("acthi_done")
        actlo_done = sem("actlo_done")
        par_in = sem("par_in")
        par_t = sem("par_t")
        par_done = sem("par_done")
        wab_in = sem("wab_in")
        abhi_done = sem("abhi_done")
        ablo_done = sem("ablo_done")
        ab_pe = sem("ab_pe")
        ab_v = sem("ab_v")
        ab_a = sem("ab_a")
        taps = sem("taps")
        csq_done = sem("csq_done")
        cf_done = sem("cf_done")
        cth_done = sem("cth_done")
        cn_done = sem("cn_done")
        cp_done = sem("cp_done")
        ab_h = sem("ab_h")
        hn_done = sem("hn_done")
        chi_done = sem("chi_done")
        clo_done = sem("clo_done")
        th_done = sem("th_done")
        ta_done = sem("ta_done")
        mg_done = sem("mg_done")
        mghi_done = sem("mghi_done")
        mglo_done = sem("mglo_done")
        fin_t = sem("fin_t")
        fin_y = sem("fin_y")
        stored = sem("stored")
        pe_dn = Steps(sem("pe_dn"), PE_STEPS)
        ve_dn = Steps(sem("ve_dn"), DVE_STEPS)
        ac_dn = Steps(sem("ac_dn"), ACT_STEPS)
        po_dn = Steps(sem("po_dn"), POOL_STEPS)
        ac_ds = Steps(sem("ac_ds"), ACT_DENSE)
        ve_ds = Steps(sem("ve_ds"), DVE_DENSE)

        block = ctx.enter_context(nc.Block())
        X_TILES = 8 + 24 * DEPTH

        def chunked(t):
            return t[:, :].rearrange("p (c i) -> p c i", c=NC)

        def each_chunk(i):
            return cst[:, i:i + 1, :].broadcast_to([P, NC, P])

        def spread(cols):
            return cols.rearrange("p (c o) -> p c o", o=1).broadcast_to([P, NC, P])

        @block.sync
        def _(sp):
            sp.dma_start(cst[:, :, :], consts).then_inc(const_in, 16)
            for k in range(NC):
                sp.dma_start(raw[k][:, :], x[0, k * P:(k + 1) * P, :]).then_inc(const_in, 16)
            w_in_v = w_in.rearrange("l (k p) c -> l p k c", p=P)

            def unit(Rd, own, mine, c, src, kts=KT):
                if mine is not None:
                    sp.wait_ge(mine, own * 4 + (c + 1))
                dst = raw[c % SLOTS][:, 0:kts * P].rearrange("p (k c) -> p k c", k=kts)
                sp.dma_start(dst, src).then_inc(raw_landed[c % SLOTS], 16)

            def ffn_units(l, w_gate, w_up, w_down, r_f, v_f, r_d, v_d):
                wg, wu, wd = (w.rearrange("l (k p) c -> l p k c", p=P) for w in (w_gate, w_up, w_down))
                with sp.Fori(0, FT // 2) as i:
                    for c in range(4):
                        src = (wg, wu)[c % 2][l, :, :, ds(i * 256 + (c // 2) * P, P)]
                        unit(l * R_LAYER + i + r_f, l * V_LAYER + i + v_f, lo_v, c, src)
                with sp.Fori(0, 2) as i:
                    for c in range(12):
                        a, b = DSPLIT[c % 3]
                        src = wd[l, :, a:b, ds(i * 512 + (c // 3) * P, P)]
                        unit(l * R_LAYER + i * 3 + r_d, l * V_LAYER + i * 3 + v_d, lo_v, c, src, b - a)

            sp.wait_ge(init, 4)
            with sp.Fori(0, DEPTH) as l:
                sp.wait_ge(par_t, l + 1)
                sp.dma_start(prow[PR_DW:PR_DW + TAPS, :], dw_conv_w[l]).then_inc(par_in, 16)
                for row, v in ((PR_B, dw_conv_b), (PR_CN, conv_norm), (PR_F1, ffn1_norm), (PR_MIX, mix_norm), (PR_F2, ffn2_norm)):
                    sp.dma_start(prow[row:row + 1, :], v[ds(l, 1), :]).then_inc(par_in, 16)
                for t in range(SC):
                    sp.dma_start(prow[PR_QKV + 3 * t:PR_QKV + 3 * t + 3, :],
                                 qkv_conv_w[l, t].rearrange("(q c) -> q c", q=3)).then_inc(par_in, 16)
                sp.wait_ge(xt_done, NC)
                ffn_units(l, ffn1_w_gate, ffn1_w_up, ffn1_w_down, R_F1, V_F1, R_D1, V_D1)
                sp.wait_ge(lo_v, l * (V_LAYER * 4) + (V_T * 4 + SLOTS))
                head_cols = (C_Q, C_K, C_V, C_G, C_VAL, C_GT)

                def head_units(hd, Rd, G, c0, ts=range(6)):
                    for t in ts:
                        unit(Rd, G, None if c0 + t < SLOTS else lo_g, c0 + t, w_in_v[l, :, :, ds(hd * P + head_cols[t], P)])

                head_units(0, l * R_LAYER + R_H, l * G_LAYER, 0, range(SLOTS))
                sp.wait_ge(x_upd, l * 24 + 16)
                sp.dma_start(wab_raw[:, :, :], w_in_v[l, :, :, C_AB:C_AB + 16]).then_inc(wab_in, 16)
                sp.dma_start(alb[:, 0, :], a_log[ds(l, 1), :].broadcast_to([P, HEADS])).then_inc(wab_in, 16)
                sp.dma_start(alb[:, 1, :], dt_bias[ds(l, 1), :].broadcast_to([P, HEADS])).then_inc(wab_in, 16)
                sp.dma_start(hnw[:, :], head_norm[l].rearrange("(p o) -> p o", o=1)).then_inc(wab_in, 16)
                head_units(0, l * R_LAYER + R_H, l * G_LAYER, 0, range(SLOTS, 6))
                with sp.Fori(0, 3) as p:
                    for half in range(2):
                        head_units(p * 2 + (1 + half), l * R_LAYER + p * 3 + R_H, l * G_LAYER + p * 3, 6 + 6 * half)
                head_units(7, l * R_LAYER + (R_H + 9), l * G_LAYER + 9, 6)
                wa, wb, wo = (w.rearrange("l (k p) c -> l p k c", p=P) for w in (w_a_out, w_b_out, w_o))
                with sp.Fori(0, KT) as m:
                    for c, src in enumerate((w_in_v[l, :, :, ds(m * P + C_GA, P)], w_in_v[l, :, :, ds(m * P + C_GB, P)],
                                             wa[l, :, :, ds(m * P, P)], wb[l, :, :, ds(m * P, P)])):
                        if c == 0:
                            sp.wait_ge(lo_g, (l + 1) * (G_LAYER * 4) + SLOTS)
                        unit(l * R_LAYER + m + R_T, l * V_LAYER + m + V_T, lo_v, c, src)
                with sp.Fori(0, 2) as i:
                    for c in range(4):
                        unit(l * R_LAYER + i + R_O, l * V_LAYER + i + V_O, lo_v, c, wo[l, :, :, ds(i * 512 + c * P, P)])
                ffn_units(l, ffn2_w_gate, ffn2_w_up, ffn2_w_down, R_F2, V_F2, R_D2, V_D2)
            sp.wait_ge(par_t, DEPTH + 1)
            sp.dma_start(prow[:, :], final_norm.rearrange("(o c) -> o c", o=1).broadcast_to([P, D])).then_inc(par_in, 16)
            for c in range(NC):
                for half in range(2):
                    sp.wait_ge(fin_y, 2 * c + half + 1)
                    sp.dma_start(out[0, c * P:(c + 1) * P, half * 512:half * 512 + 512],
                                 raw[c][:, half * 512:half * 512 + 512]).then_inc(stored, 16)
            sp.wait_ge(stored, 16 * 2 * NC)

        @block.tensor
        def _(pe):
            def mm(o, a, b, start=True, stop=True, **kw):
                return nc.tensor.matmul(o, a, b, start=start, stop=stop, **kw)

            def three(bk, slot, kk, a_hi, a_lo, k, first, last, only=None):
                w = slice(kk * P, kk * P + P)
                r = None
                for j, (wt, at) in enumerate(((w_hi, a_hi), (w_hi, a_lo), (w_lo, a_hi))):
                    if only is None or only == j:
                        r = mm(bank[bk][:, :], wt[slot][:, w], at[:, k, :], start=first and j == 0, stop=last and j == 2)
                return r

            def norm_stats(rn):
                pe.wait_ge(ssq_done, rn * 6 + 6)
                pe.wait_ge(sq_done, rn * 8 + 8)
                for c in range(NC):
                    mm(bank[6][:, c:c + 1], ssq[:, c * P:c * P + P], ones[:, 0:1], stop=False)
                    m = mm(bank[6][:, c:c + 1], sqb[(KT - 1) % 2][:, c * P:c * P + P], ones[:, 0:1], start=False)
                m.then_inc(stat, 1)

            def norm_spread(nf):
                pe.wait_ge(fbc_done, nf + 1)
                for c in range(NC):
                    m = mm(bank[7][:, c * P:c * P + P], fbc[:, c, :], ident)
                m.then_inc(bc, 1)

            def ffn(l, w, r_f, v_f, r_d, v_d, nrm_i, nf, base_upd):
                norm_stats(l * 3 + nrm_i)
                norm_spread(nf)
                with pe.Fori(0, FT // 2) as i:
                    for c in range(4):
                        pe.wait_ge(lo_v, l * (V_LAYER * 4) + i * 4 + (v_f * 4 + c + 1 + SLOTS))
                        done = silu_done if c % 2 == 0 else prod_done
                        pe.wait_ge(done, l * (2 * FT) + i * 2 + (w * FT + c // 2 + 1))
                        for k in range(KT):
                            if c == 0:
                                pe.wait_ge((hlo_g, hlo_v)[k % 2], l * 12 + (nrm_i * 4 + k // 2 + 1))
                            m = three(c, c, k, h_hi, h_lo, k, k == 0, k == KT - 1)
                        m.then_inc(used, 1)
                with pe.Fori(0, 2) as i:
                    for j in range(4):
                        pe.wait_ge(x_upd, l * 24 + i * 4 + (base_upd + j - 1))
                        for q in range(3):
                            c = 3 * j + q
                            pe.wait_ge(lo_v, l * (V_LAYER * 4) + i * 12 + (v_d * 4 + c + 1 + SLOTS))
                            a, b = DSPLIT[q]
                            for k in range(a, b):
                                if j == 0:
                                    pe.wait_ge(actlo_done, l * (2 * FT) + (w * FT + k + 1))
                                m = three(4 + j % 2, c % SLOTS, k - a, act_hi, act_lo, k, k == 0, k == FT - 1)
                            m.then_inc(used, 1)

            pe.wait_ge(const_in, 16 * (1 + NC))
            pe.wait_ge(init, 4)
            for c in range(NC):
                for k in range(KT):
                    m = nc.tensor.transpose(bank[k][:, c * P:c * P + P], raw[c][:, k * P:k * P + P], ident)
                m.then_inc(xt_done, 1)

            with pe.Fori(0, DEPTH) as l:
                pe.wait_ge(par_in, l * 160 + 160)
                pe.wait_ge(x_upd, l * 24 + 8)
                for k in range(KT):
                    m = nc.tensor.transpose(bank[4 + k // 4][:, k % 4 * P:k % 4 * P + P], prow[:, k * P:k * P + P], ident)
                m.then_inc(par_t, 1)
                ffn(l, 0, R_F1, V_F1, R_D1, V_D1, 0, l * 4, 8)

                norm_stats(l * 3 + 1)
                norm_spread(l * 4 + 1)
                pe.wait_ge(ablo_done, l + 1)
                for k in range(KT):
                    pe.wait_ge((hlo_g, hlo_v)[k % 2], l * 12 + (4 + k // 2 + 1))
                    for j, (wt, at) in enumerate(((wab_hi, h_hi), (wab_hi, h_lo), (wab_lo, h_hi))):
                        m = mm(bank[0][0:16, :], wt[:, k, :], at[:, k, :], start=(k == 0 and j == 0), stop=(k == KT - 1 and j == 2))
                m.then_inc(ab_pe, 1)

                def ab_turn():
                    pe.wait_ge(ab_v, l * AB_V + 1)
                    for c in range(NC):
                        m = mm(bank[1][:, c * 16:c * 16 + 16], abT[0:16, c * P:c * P + P], cst[0:16, I_ID, 0:16])
                    m.then_inc(ab_pe, 1)

                def ab_sums():
                    pe.wait_ge(ab_v, l * AB_V + AB_G)
                    mm(bank[1][:, 0:32], incl, hsc[:, :, HS_G, :])
                    mm(bank[1][:, 32:64], ones[:, :], hsc[:, :, HS_G, :]).then_inc(ab_pe, 1)

                def dense_quarter(s, Rg, c0, rd):
                    t, part = divmod(s, 6)
                    slot = (c0 + t) % SLOTS
                    if part == 0:
                        pe.wait_ge(lo_g, Rg * 4 + (c0 + t + 1 + SLOTS))
                        if t == 0:
                            pe.wait_ge(ac_ds.sem, ac_ds.after(rd - 1, "val"))
                        if t == 1:
                            pe.wait_ge(ac_ds.sem, ac_ds.after(rd - 1, "gt_th"))
                        if t in (2, 3, 4):
                            pe.wait_ge(ac_ds.sem, ac_ds.after(rd, ("q_tap", "k_tap", "v_tap")[t - 2]))
                        if t == 5:
                            pe.wait_ge(ve_ds.sem, ve_ds.after(rd, "sg"))
                    for n in range(4 * part, 4 * part + 4):
                        k, j = divmod(n, 3)
                        m = three(6 + t % 2, slot, k, h_hi, h_lo, k, k == 0, k == KT - 1, only=j)
                    if part == 5:
                        m.then_inc(used, 1)

                def each(o, a, b, name):
                    for c in range(NC):
                        m = mm(o[:, c * P:c * P + P], a[:, c * P:c * P + P], b[:, c * P:c * P + P])
                    m.then_inc(*pe_dn.step(name))

                def turn(o, a, name):
                    for c in range(NC):
                        m = nc.tensor.transpose(o[:, c * P:c * P + P], a[:, c * P:c * P + P], ident)
                    m.then_inc(*pe_dn.step(name))

                def stage(name, rn):
                    def ve(n, r=rn):
                        pe.wait_ge(ve_dn.sem, ve_dn.after(r, n))

                    def ac(n, r=rn):
                        pe.wait_ge(ac_dn.sem, ac_dn.after(r, n))

                    if name == "gr":
                        ve("gbc")
                        for c in range(NC):
                            m = mm(bank[0][:, c * P:c * P + P], dec[:, c * P:c * P + P], incl)
                        m.then_inc(*pe_dn.step(name))
                    elif name == "kt":
                        ve("kT")
                        turn(bank[1], kT, name)
                    elif name == "kk":
                        each(bank[2], kT, kT, name)
                    elif name == "sk":
                        ac("ksq")
                        ve("olo", rn - 1)
                        for c in range(NC):
                            m = mm(bank[5][:, c:c + 1], NT[:, c * P:c * P + P], ones[:, 0:1])
                        m.then_inc(*pe_dn.step(name))
                    elif name == "kq":
                        ve("qT")
                        each(bank[3], kT, qT, name)
                    elif name == "vt":
                        ve("vT")
                        turn(bank[4], va, name)
                    elif name == "x2t":
                        ve("x2T")
                        ac("eg")
                        turn(bank[0], XT, name)
                    elif name[0] == "y":
                        lv = int(name[1:])
                        ac("X2" if lv == 0 else f"XT{lv - 1}")
                        ac("kd")
                        if lv:
                            ve(f"x{lv - 1}")
                        each(bank[1], NT, X, name)
                    elif name[:2] == "xy":
                        pass
                    elif name[:2] == "xt":
                        lv = int(name[2:])
                        ve(f"x{lv}")
                        ve("attnT")
                        turn(bank[3], X, name)
                    elif name[:2] == "vn":
                        c = int(name[2:])
                        ac("vs")
                        if c:
                            ve(f"r{c}")
                        else:
                            ve(f"x{LEVELS - 1}")
                        mm(bank[1][:, 0:P], XT[:, c * P:c * P + P], (R[:, :] if c else vs[:, 0:P])).then_inc(*pe_dn.step(name))
                    elif name[:2] == "os":
                        c = int(name[2:])
                        t = slice(c * P, c * P + P)
                        ve(f"vn{c}")
                        pe.wait_ge(po_dn.sem, po_dn.after(rn, "qd"))
                        if c:
                            mm(bank[4][:, t], S[:, :], qd[:, t], stop=False)
                        m = mm(bank[4][:, t], VN[:, :], attn[:, t], start=(c == 0))
                        if c < NC - 1:
                            m = mm(bank[2][:, 0:P], kd[:, t], VN[:, :])
                        m.then_inc(*pe_dn.step(name))
                    elif name[0] == "p":
                        c = int(name[1:])
                        ve(f"s{c - 1}")
                        mm(bank[0][:, 0:P], kT[:, c * P:c * P + P], S[:, :]).then_inc(*pe_dn.step(name))
                    elif name == "so":
                        ac("osq")
                        for c in range(NC):
                            mm(bank[5][:, c:c + 1], X[:, c * P:c * P + P], ones[:, 0:1], stop=False)
                            m = mm(bank[5][:, c:c + 1], Y[:, c * P:c * P + P], ones[:, 0:1], start=False)
                        m.then_inc(*pe_dn.step(name))
                    elif name == "fb":
                        ve("fbc")
                        for c in range(NC):
                            m = mm(bank[3][:, c * P:c * P + P], decs[:, c * P:c * P + P], ident)
                        m.then_inc(*pe_dn.step(name))

                def xy(lv, rn):
                    pe.wait_ge(ve_dn.sem, ve_dn.after(rn, f"y{lv}"))
                    if lv < LEVELS - 1:
                        each(bank[2], XT, Y, f"xy{lv}")
                    else:
                        each(bank[2], Y, XT, f"xy{lv}")

                def run_stage(name, rn):
                    if name.startswith("xy"):
                        xy(int(name[2:]), rn)
                    else:
                        stage(name, rn)

                def head(dense, rn):
                    for s in range(36):
                        if dense:
                            dense_quarter(s, *dense)
                        if rn is None and s == 3:
                            ab_turn()
                        if rn is not None and s >= 1:
                            run_stage(PE_STEPS[s - 1], rn)
                    if rn is not None:
                        for name in PE_STEPS[35:]:
                            run_stage(name, rn)

                G0 = l * G_LAYER
                head((G0, 0, l * 8), None)
                ab_sums()
                with pe.Fori(0, 3) as p:
                    for half in range(2):
                        head((G0 + p * 3, 6 + 6 * half, l * 8 + p * 2 + (1 + half)), l * 8 + p * 2 + half)
                head((G0 + 9, 6, l * 8 + 7), l * 8 + 6)
                head(None, l * 8 + 7)

                pe.wait_ge(csq_done, l * 7 + 7)
                for c in range(NC):
                    m = mm(bank[6][:, c:c + 1], ssq[:, c * P:c * P + P], ones[:, 0:1])
                m.then_inc(stat, 1)
                norm_spread(l * 4 + 2)

                with pe.Fori(0, KT) as m_:
                    for c in range(4):
                        pe.wait_ge(lo_v, l * (V_LAYER * 4) + m_ * 4 + (V_T * 4 + c + 1 + SLOTS))
                        if c < 2:
                            pe.wait_ge(th_done, l * 16 + m_ * 2 + (c + 1))
                        else:
                            pe.wait_ge(ta_done, l * 16 + m_ * 2 + (c - 2 + 1))
                        if c == 2:
                            pe.wait_ge(ve_dn.sem, ve_dn.after(l * 8 + 7, "olo"))
                        for k in range(KT):
                            if c == 3:
                                pe.wait_ge(clo_done, l * 8 + (k + 1))
                            a_hi, a_lo = ((h_hi, h_lo), (h_hi, h_lo), (o_hi, o_lo), (c_hi, c_lo))[c]
                            m = three(c, c, k, a_hi, a_lo, k, k == 0, k == KT - 1)
                        m.then_inc(used, 1)
                with pe.Fori(0, 2) as i:
                    for j in range(4):
                        pe.wait_ge(lo_v, l * (V_LAYER * 4) + i * 4 + (V_O * 4 + j + 1 + SLOTS))
                        pe.wait_ge(x_upd, l * 24 + i * 4 + (16 + j - 1))
                        for k in range(KT):
                            if j == 0:
                                pe.wait_ge(mglo_done, l * 8 + (k + 1))
                            m = three(4 + j % 2, j, k, mg_hi, mg_lo, k, k == 0, k == KT - 1)
                        m.then_inc(used, 1)
                ffn(l, 1, R_F2, V_F2, R_D2, V_D2, 2, l * 4 + 3, 24)

            norm_stats(3 * DEPTH)
            for c in range(NC):
                for half in range(2):
                    n = 2 * c + half
                    if n >= 2:
                        pe.wait_ge(fin_y, n - 1)
                    for k in range(4):
                        m = nc.tensor.transpose(bank[n % 2][:, k * P:k * P + P], xT[:, 4 * half + k, c * P:c * P + P], ident)
                    m.then_inc(fin_t, 1)


        @block.scalar
        def _(act):
            def hi(Rd, c):
                act.wait_ge(raw_landed[c % SLOTS], Rd * 16 + 16 * (c // SLOTS + 1))
                act.wait_ge(used, Rd * 4 + (c + 1))
                nc.scalar.activation(w_hi[c % SLOTS][:, :], raw[c % SLOTS][:, :], ACT.Copy).then_inc(hi_done, 1)

            def square_x(rn, m, upd):
                act.wait_ge(x_upd, upd)
                if m >= 3:
                    act.wait_ge(ssq_done, rn * 6 + (m - 2))
                dst = ssq if m == 0 else sqb[m % 2]
                nc.scalar.activation(dst[:, :], xT[:, m, :], ACT.Square).then_inc(sq_done, 1)

            def norm_hi(nh):
                for k in range(KT):
                    act.wait_ge(hf_done, nh * 8 + (k + 1))
                    nc.scalar.activation(h_hi[:, k, :], hb[k % 4][:, :], ACT.Copy).then_inc(hhi_done, 1)

            def ffn(l, w, r_f, r_d, nrm_i, upd0):
                norm_hi(l * 3 + nrm_i)
                with act.Fori(0, FT // 2) as i:
                    Rd = l * R_LAYER + i + r_f
                    for c in range(4):
                        if c % 2 == 0:
                            act.wait_ge(used, Rd * 4 + (c + 1 + SLOTS))
                            act.wait_ge(prod_done, l * (2 * FT) + i * 2 + (w * FT + c // 2 + 1))
                            nc.scalar.activation(sg_f[c // 2][:, :], bank[c][:, :], ACT.Silu).then_inc(silu_done, 1)
                        hi(Rd, c + 4)
                for i in range(2):
                    for c in range(12):
                        last = i == 1 and c == 11
                        if not last and not (w == 1 and i == 1 and c >= 8):
                            hi(l * R_LAYER + (r_d + 3 * i), c + 4)
                        if c % 3 == 2:
                            m = 4 * i + c // 3
                            square_x(l * 3 + nrm_i + 1, m, l * 24 + (upd0 + m + 1))
                        if last and w == 0:
                            hi(l * R_LAYER + (r_d + 3 * i), c + 4)

            for m in range(KT):
                square_x(0, m, m + 1)
            with act.Fori(0, DEPTH) as l:
                for c in range(4):
                    hi(l * R_LAYER, c)
                ffn(l, 0, R_F1, R_D1, 0, 8)
                act.wait_ge(wab_in, l * 64 + 64)
                nc.scalar.activation(wab_hi[:, :, :], wab_raw[:, :, :], ACT.Copy).then_inc(abhi_done, 1)
                norm_hi(l * 3 + 1)
                act.wait_ge(ab_v, l * AB_V + 4)
                nc.scalar.activation(abw[:, 1, :, :], abw[:, 1, :, :], ACT.Exp, scale=-1.0).then_inc(ab_a, 1)
                nc.scalar.activation(abw[:, 5, :, :].rearrange("p h c -> p c h"), ab[:, :, 8:16], ACT.Tanh, scale=0.5).then_inc(ab_a, 1)
                nc.scalar.activation(alb[:, 0, :], alb[:, 0, :], ACT.Exp).then_inc(ab_a, 1)

                def ab_exps():
                    act.wait_ge(ab_v, l * AB_V + AB_G + 1)
                    act.wait_ge(ab_pe, l * 3 + 3)
                    nc.scalar.activation(abw[:, 2, :, :], hsc[:, :, HS_GC, :], ACT.Exp).then_inc(ab_a, 1)
                    nc.scalar.activation(hsc[:, :, HS_KD, :], abw[:, 0, :, :], ACT.Exp).then_inc(ab_a, 1)
                    nc.scalar.activation(hsc[:, :, HS_GL, :], abw[:, 3, :, :], ACT.Exp).then_inc(ab_a, 1)

                def dense_steps(t, Rd, c0, rd):
                    act.wait_ge(used, Rd * 4 + (c0 + t + 1 + SLOTS))
                    bk = bank[6 + t % 2]
                    if t < 3:
                        n, dst, acc = (("q", q_raw, qa), ("k", k_raw, ka), ("v", v_raw, va))[t]
                        act.wait_ge(ve_ds.sem, ve_ds.after(rd - 1, f"{n}3"))
                        nc.scalar.activation(dst[:, SC - 1:], bk[:, :], ACT.Copy).then_inc(*ac_ds.step(f"{n}_raw"))
                        act.wait_ge(ve_dn.sem, ve_dn.after(rd - 1, f"{n}T"))
                        if n == "v":
                            act.wait_ge(pe_dn.sem, pe_dn.after(rd - 1, "vt"))
                        act.wait_ge(ve_ds.sem, ve_ds.after(rd, "dcol"))
                        w = PR_QKV + 3 * (SC - 1) + t
                        nc.scalar.activation(acc[:, :], bk[:, :], ACT.Copy, scale=dcol[:, w:w + 1]).then_inc(*ac_ds.step(f"{n}_tap"))
                    elif t == 3:
                        act.wait_ge(ve_ds.sem, ve_ds.after(rd - 1, "craw"))
                        nc.scalar.activation(gth[:, :], bk[:, :], ACT.Tanh, scale=0.5).then_inc(*ac_ds.step("g_th"))
                    elif t == 4:
                        act.wait_ge(ve_ds.sem, ve_ds.after(rd - 1, "craw"))
                        nc.scalar.activation(valb[:, :], bk[:, :], ACT.Copy).then_inc(*ac_ds.step("val"))
                    else:
                        act.wait_ge(ve_ds.sem, ve_ds.after(rd, "sg"))
                        nc.scalar.activation(gth[:, :], bk[:, :], ACT.Tanh, scale=0.5).then_inc(*ac_ds.step("gt_th"))
                    hi(Rd, c0 + t + 4)

                def dn_steps(part, rn):
                    def ve(n, r=rn):
                        act.wait_ge(ve_dn.sem, ve_dn.after(r, n))

                    def pe_(n, r=rn):
                        act.wait_ge(pe_dn.sem, pe_dn.after(r, n))

                    if part == 0:
                        act.wait_ge(ve_ds.sem, ve_ds.after(rn, "sg"))
                        ve("og", rn - 1)
                        nc.scalar.activation(sgc[:, :], sgn[:, :], ACT.Copy).then_inc(*ac_dn.step("sgc"))
                        pe_("so", rn - 1)
                        act.wait_ge(ve_ds.sem, ve_ds.after(rn, "v3"))
                        nc.scalar.activation(Y[:, :], ka[:, :], ACT.Tanh).then_inc(*ac_dn.step("thk"))
                        nc.scalar.activation(X[:, :], qa[:, :], ACT.Tanh).then_inc(*ac_dn.step("thq"))
                        nc.scalar.activation(XT[:, :], va[:, :], ACT.Tanh).then_inc(*ac_dn.step("thv"))
                        ve("kT")
                        nc.scalar.activation(NT[:, :], kT[:, :], ACT.Square).then_inc(*ac_dn.step("ksq"))
                        ve("dmin")
                        nc.scalar.activation(qd[:, :], bank[0][:, :], ACT.Exp).then_inc(*ac_dn.step("eg"))
                        nc.scalar.activation(dec[:, :], dec[:, :], ACT.Exp).then_inc(*ac_dn.step("decT"))
                        pe_("kt")
                        for c in range(NC):
                            a = nc.scalar.activation(kd[:, c * P:c * P + P], bank[1][:, c * P:c * P + P], ACT.Copy, scale=hs[:, HS_KD, c:c + 1])
                        a.then_inc(*ac_dn.step("kd"))
                    elif part == 1:
                        pe_("vt")
                        act.wait_ge(po_dn.sem, po_dn.after(rn, "rk"))
                        for c in range(NC):
                            a = nc.scalar.activation(vs[:, c * P:c * P + P], bank[4][:, c * P:c * P + P], ACT.Copy, scale=sm[:, 3, c:c + 1])
                        a.then_inc(*ac_dn.step("vs"))
                        pe_("x2t")
                        nc.scalar.activation(X[:, :], bank[0][:, :], ACT.Copy).then_inc(*ac_dn.step("X2"))
                    elif part < 2 + LEVELS - 1:
                        lv = part - 2
                        pe_(f"xt{lv}")
                        nc.scalar.activation(XT[:, :], bank[3][:, :], ACT.Copy).then_inc(*ac_dn.step(f"XT{lv}"))
                    else:
                        pe_("xy5")
                        nc.scalar.activation(X[:, :], qT[:, :], ACT.Square, scale=float(np.sqrt(P * EPS))).then_inc(*ac_dn.step("qsq"))
                        pe_("os3")
                        nc.scalar.activation(Y[:, :], bank[4][:, :], ACT.Square, scale=float(np.sqrt(1.0 / P))).then_inc(*ac_dn.step("osq"))

                def head(dense, rn):
                    order = [("n", 0), ("d", 0), ("n", 1), ("n", 2), ("d", 1), ("n", 3), ("n", 4), ("d", 2), ("n", 5), ("n", 6),
                             ("d", 3), ("d", 4), ("d", 5), ("n", 7)]
                    for kind, n in order:
                        if kind == "d" and dense:
                            dense_steps(n, *dense)
                        if kind == "n" and rn is not None:
                            dn_steps(n, rn)

                Rh = l * R_LAYER + R_H
                head((Rh, 0, l * 8), None)
                ab_exps()
                with act.Fori(0, 3) as p:
                    for half in range(2):
                        head((Rh + p * 3, 6 + 6 * half, l * 8 + p * 2 + (1 + half)), l * 8 + p * 2 + half)
                head((Rh + 9, 6, l * 8 + 7), l * 8 + 6)
                head(None, l * 8 + 7)
                for m in range(KT):
                    if m == 0:
                        act.wait_ge(taps, l * (8 * TAPS) + 9 * TAPS)
                        act.wait_ge(ve_dn.sem, ve_dn.after(l * 8 + 7, "olo"))
                    if m >= 3:
                        act.wait_ge(csq_done, l * 7 + (m - 2))
                    dst = ssq if m == 0 else sqb[m % 2]
                    nc.scalar.activation(dst[:, :], c_all[:, m, :], ACT.Square).then_inc(cf_done, 1)
                for k in range(KT):
                    if k == 0:
                        act.wait_ge(cn_done, l * 8 + 1)
                        nc.scalar.activation(cth[0][:, :], hf[0][:, :], ACT.Tanh).then_inc(cth_done, 1)
                    if k < KT - 1:
                        act.wait_ge(cn_done, l * 8 + (k + 2))
                        nc.scalar.activation(cth[(k + 1) % 2][:, :], hf[(k + 1) % 2][:, :], ACT.Tanh).then_inc(cth_done, 1)
                    act.wait_ge(cp_done, l * 8 + (k + 1))
                    nc.scalar.activation(c_hi[:, k, :], hf[k % 2][:, :], ACT.Copy).then_inc(chi_done, 1)
                with act.Fori(0, KT) as m:
                    Rd = l * R_LAYER + m + R_T
                    for c in range(4):
                        if c < 2:
                            act.wait_ge(used, Rd * 4 + (c + 1 + SLOTS))
                            act.wait_ge(clo_done, l * 8 + 8)
                            act.wait_ge(ta_done, l * 16 + m * 2 + (c + 1))
                            nc.scalar.activation((thA, thB)[c][:, :], bank[c][:, :], ACT.Tanh, scale=0.5).then_inc(th_done, 1)
                        hi(Rd, c + 4)
                for k in range(KT):
                    if k == 0:
                        act.wait_ge(used, l * (R_LAYER * 4) + ((R_T + KT - 1) * 4 + 3 + SLOTS))
                    act.wait_ge(mg_done, l * 8 + (k + 2))
                    nc.scalar.activation(mg_hi[:, k, :], mg[:, k, :], ACT.Copy).then_inc(mghi_done, 1)
                for i in range(2):
                    for c in range(4):
                        hi(l * R_LAYER + (R_O + i), c + 4)
                        square_x(l * 3 + 2, 4 * i + c, l * 24 + (16 + 4 * i + c + 1))
                ffn(l, 1, R_F2, R_D2, 2, 24)

        @block.vector
        def _(dve):
            tt, ts, stt = nc.vector.tensor_tensor, nc.vector.tensor_scalar, nc.vector.scalar_tensor_tensor

            def lo(Rd, Vd, c):
                dve.wait_ge(hi_done, Rd * 4 + (c + 1))
                tt(w_lo[c % SLOTS][:, :], raw[c % SLOTS][:, :], w_hi[c % SLOTS][:, :].bitcast(F32), ALU.subtract).then_inc(lo_v, 1)

            def norm_factor(rn, nf):
                dve.wait_ge(stat, nf + 1)
                ts(nrm[:, 0, :], bank[6][:, 0:NC], 1.0 / D, EPS, ALU.mult, ALU.add).then_inc(var_done, 1)

            def norm_fbc(nf):
                dve.wait_ge(rs_done, nf + 1)
                nc.vector.tensor_copy(fbc[:, :, :], spread(nrm[:, 1, :])).then_inc(fbc_done, 1)

            def norm_h(nh, nf, row):
                norm_factor(nh, nf)
                norm_fbc(nf)
                dve.wait_ge(bc, nf + 1)
                for k in range(KT + 1):
                    if k < KT:
                        if k >= 4:
                            dve.wait_ge((hlo_g, hlo_v)[k % 2], nh * 4 + ((k - 4) // 2 + 1))
                        stt(out=hb[k % 4][:, :], in0=xT[:, k, :], scalar=pcol[:, k, row:row + 1], in1=bank[7][:, :],
                            op0=ALU.mult, op1=ALU.mult).then_inc(hf_done, 1)
                    if k and k % 2 == 0:
                        dve.wait_ge(hhi_done, nh * 8 + k)
                        tt(h_lo[:, k - 1, :], hb[(k - 1) % 4][:, :], h_hi[:, k - 1, :].bitcast(F32), ALU.subtract).then_inc(hlo_v, 1)

            def add_x(m, Rd, c, upd, scale, bk):
                dve.wait_ge(used, Rd * 4 + (c + 1 + SLOTS))
                stt(out=xT[:, m, :], in0=bank[bk][:, :], scalar=scale, in1=xT[:, m, :], op0=ALU.mult, op1=ALU.add).then_inc(x_upd, 1)

            def ffn(l, w, r_f, v_f, r_d, v_d, nrm_i, nf, row):
                norm_h(l * 3 + nrm_i, nf, row)
                with dve.Fori(0, FT // 2) as i:
                    Rd, Vd = l * R_LAYER + i + r_f, l * V_LAYER + i + v_f
                    for c in range(4):
                        if c % 2:
                            f = c // 2
                            n = l * (2 * FT) + i * 2 + (w * FT + f)
                            dve.wait_ge(used, Rd * 4 + (c + 1 + SLOTS))
                            dve.wait_ge(silu_done, n + (1 + 2))
                            tt(a_f[f][:, :], sg_f[f][:, :], bank[c][:, :], ALU.mult).then_inc(prod_done, 1)
                            dve.wait_ge(prod_done, n + (1 + 2))
                            ts(act_hi[:, i * 2 + f, :], a_f[f][:, :], 1.0, None, ALU.mult).then_inc(acthi_done, 1)
                            dve.wait_ge(acthi_done, n + 1)
                            tt(act_lo[:, i * 2 + f, :], a_f[f][:, :], act_hi[:, i * 2 + f, :].bitcast(F32), ALU.subtract).then_inc(actlo_done, 1)
                        lo(Rd, Vd, c + 4)
                for i in range(2):
                    for c in range(12):
                        if not (i == 1 and c >= 8):
                            lo(l * R_LAYER + (r_d + 3 * i), None, c + 4)
                        if c % 3 == 2:
                            add_x(4 * i + c // 3, l * R_LAYER + (r_d + 3 * i), c, None, 0.5, 4 + (c // 3) % 2)

            nc.vector.memset(ones[:, :], 1.0).then_inc(init, 1)
            nc.vector.memset(pw[:, 0, :], -0.5).then_inc(init, 1)
            nc.vector.memset(pw[:, 1, :], 0.5).then_inc(init, 1)
            nc.vector.memset(prow[:, :], 0.0).then_inc(init, 1)
            dve.wait_ge(xt_done, NC)
            for k in range(KT):
                nc.vector.tensor_copy(xT[:, k, :], bank[k][:, :]).then_inc(x_upd, 1)

            with dve.Fori(0, DEPTH) as l:
                for c in range(4):
                    lo(l * R_LAYER, None, c)
                dve.wait_ge(par_t, l + 2)
                for a, b, f in ((PR_DW, PR_B, 0.5), (PR_B, PR_CN, 1.0), (PR_CN, PR_F1, 0.5), (PR_F1, PR_QKV, 1.0), (PR_QKV, PR_N, 0.5)):
                    for half in range(2):
                        pv = bank[4 + half][:, :].rearrange("p (k r) -> p k r", k=4)
                        last = ts(pcol[:, 4 * half:4 * half + 4, a:b], pv[:, :, a:b], f, None, ALU.mult)
                last.then_inc(par_done, 1)
                dve.wait_ge(par_done, l + 1)
                ffn(l, 0, R_F1, V_F1, R_D1, V_D1, 0, l * 4, PR_F1)

                dve.wait_ge(abhi_done, l + 1)
                tt(wab_lo[:, :, :], wab_raw[:, :, :], wab_hi[:, :, :].bitcast(F32), ALU.subtract).then_inc(ablo_done, 1)
                for r in (q_raw, k_raw, v_raw):
                    nc.vector.memset(r[:, 0:SC - 1], 0.0)
                nc.vector.memset(c_raw[:, 0:TAPS - 1], 0.0).then_inc(init, 1)
                norm_h(l * 3 + 1, l * 4 + 1, PR_MIX)
                n = [0]

                def ab_step(ins):
                    n[0] += 1
                    ins.then_inc(ab_v, 1)
                    dve.wait_ge(ab_v, l * AB_V + n[0])

                dve.wait_ge(ab_pe, l * 3 + 1)
                ab_step(nc.vector.tensor_copy(abT[0:16, :], bank[0][0:16, :]))
                dve.wait_ge(ab_pe, l * 3 + 2)
                ab_step(nc.vector.tensor_copy(ab[:, :, :], bank[1][:, 0:NC * 16].rearrange("p (c o) -> p c o", c=NC)))
                dtb = alb[:, 1, :].rearrange("p (h o) -> p h o", o=1).broadcast_to([P, HEADS, NC])
                z, e, sv, s2, po = (abw[:, i, :, :] for i in (0, 1, 2, 3, 4))
                ab_step(tt(z, ab[:, :, 0:8].rearrange("p c h -> p h c"), dtb, ALU.add))
                ab_step(stt(out=e, in0=z, scalar=-1.0, in1=z, op0=ALU.mult, op1=ALU.max))
                dve.wait_ge(ab_a, l * 6 + 3)
                ab_step(ts(sv, e, 2.0, None, ALU.add))
                nc.vector.reciprocal(sv, sv).then_inc(ab_v, 1)
                n[0] += 1
                dve.wait_ge(ab_v, l * AB_V + n[0])
                ab_step(tt(sv, sv, e, ALU.mult))
                ab_step(tt(s2, sv, sv, ALU.mult))
                ts(po, s2, 1.0 / 17, 1.0 / 15, ALU.mult, ALU.add).then_inc(ab_h, 1)
                hcount = 1
                for q in (13, 11, 9, 7, 5, 3, 1):
                    dve.wait_ge(ab_h, l * 17 + hcount)
                    tt(po, po, s2, ALU.mult).then_inc(ab_h, 1)
                    dve.wait_ge(ab_h, l * 17 + hcount + 1)
                    ts(po, po, 1.0 / q, None, ALU.add).then_inc(ab_h, 1)
                    hcount += 2
                dve.wait_ge(ab_h, l * 17 + hcount)
                tt(po, po, sv, ALU.mult).then_inc(ab_h, 1)
                dve.wait_ge(ab_h, l * 17 + hcount + 1)
                ab_step(ts(z, z, 0.0, None, ALU.max))
                ab_step(stt(out=z, in0=po, scalar=2.0, in1=z, op0=ALU.mult, op1=ALU.add))
                ea = alb[:, 0, :].rearrange("p (h o) -> p h o", o=1).broadcast_to([P, HEADS, NC])
                ab_step(tt(z, z, ea, ALU.mult))
                ab_step(ts(hsc[:, :, HS_BETA, :], abw[:, 5, :, :], 0.5, 0.5, ALU.mult, ALU.add))
                ab_step(ts(hsc[:, :, HS_G, :], z, -1.0, None, ALU.mult))
                assert n[0] == AB_G and hcount == 15

                def ab_sums():
                    dve.wait_ge(ab_pe, l * 3 + 3)
                    sums = bank[1][:, 0:64].rearrange("p (s h c) -> p s h c", s=2, h=HEADS)
                    nc.vector.tensor_copy(hsc[:, :, HS_GC, :], sums[:, 0])
                    nc.vector.tensor_copy(abw[:, 3, :, :], sums[:, 1]).then_inc(ab_h, 1)
                    dve.wait_ge(ab_h, l * 17 + 17)
                    tt(abw[:, 0, :, :], abw[:, 3, :, :], hsc[:, :, HS_GC, :], ALU.subtract).then_inc(ab_v, 1)
                    dve.wait_ge(ab_a, l * 6 + 6)
                    ts(hsc[:, :, HS_NEG, :], abw[:, 2, :, :], -1.0, None, ALU.mult).then_inc(ab_v, 1)

                def head(dense, hn, rn, last_hi=None):
                    dn = rn is not None
                    tap = [0]

                    def fill(k):
                        if not dn:
                            return
                        for _ in range(k):
                            j = tap[0]
                            if j == TAPS:
                                return
                            tap[0] += 1
                            src = c_raw[:, j:j + SEQ]
                            if j == 0:
                                dve.wait_ge(ve_ds.sem, ve_ds.after(rn, "craw"))
                                ts(cacc[:, :], src, ncol[:, 0:1], ncol[:, PR_B:PR_B + 1], ALU.mult, ALU.add).then_inc(taps, 1)
                            else:
                                dve.wait_ge(taps, rn * TAPS + (TAPS + j))
                                dst = cacc[:, :] if j < TAPS - 1 else c_all[:, hn, :]
                                stt(out=dst, in0=src, scalar=ncol[:, j:j + 1], in1=cacc[:, :], op0=ALU.mult, op1=ALU.add).then_inc(taps, 1)

                    def ac(n, r=rn):
                        dve.wait_ge(ac_dn.sem, ac_dn.after(r, n))

                    def pe_(n, r=rn):
                        dve.wait_ge(pe_dn.sem, pe_dn.after(r, n))

                    def po_(n, r=rn):
                        dve.wait_ge(po_dn.sem, po_dn.after(r, n))

                    def me(n, r=rn):
                        dve.wait_ge(ve_dn.sem, ve_dn.after(r, n))

                    def conv(t):
                        if not dense:
                            return
                        rd = dense[2]
                        n, src, acc = (("q", q_raw, qa), ("k", k_raw, ka), ("v", v_raw, va))[t]
                        dve.wait_ge(ac_ds.sem, ac_ds.after(rd, f"{n}_tap"))
                        for j in range(SC - 1):
                            w = PR_QKV + 3 * j + t
                            if j:
                                dve.wait_ge(ve_ds.sem, ve_ds.after(rd, f"{n}{j}"))
                            stt(out=acc[:, :], in0=src[:, j:j + SEQ], scalar=dcol[:, w:w + 1], in1=acc[:, :],
                                op0=ALU.mult, op1=ALU.add).then_inc(*ve_ds.step(f"{n}{j + 1}"))
                            fill(1)

                    def level(lv):
                        pe_(f"y{lv}")
                        if lv == 0:
                            pe_("kt")
                        tt(chunked(Y), chunked(bank[1]), each_chunk(I_LV + lv), ALU.mult).then_inc(*ve_dn.step(f"y{lv}"))
                        fill(1)
                        pe_(f"xy{lv}")
                        t = X if lv < LEVELS - 1 else XT
                        tt(t[:, :], t[:, :], bank[2][:, :], ALU.subtract).then_inc(*ve_dn.step(f"x{lv}"))
                        fill(1)

                    if dense:
                        Rd, c0, rd, hd = dense
                        dve.wait_ge(ve_ds.sem, ve_ds.after(rd - 1, "v3"))
                        dve.wait_ge(ac_ds.sem, ac_ds.after(rd - 1, "v_tap"))
                        ts(dcol[:, :], pcol[:, hd, :], 1.0, None, ALU.mult).then_inc(*ve_ds.step("dcol"))
                        dve.wait_ge(ve_ds.sem, ve_ds.after(rd, "dcol"))
                    if dn:
                        dve.wait_ge(taps, rn * TAPS + TAPS)
                        me("olo", rn - 1)
                        dve.wait_ge(ab_v, (l + 1) * AB_V)
                        ts(ncol[:, :], pcol[:, hn, :], 1.0, None, ALU.mult)
                        ts(hs[:, :, :], hsc[:, hn, :, :], 1.0, None, ALU.mult).then_inc(*ve_dn.step("hs"))
                        me("hs")
                        nc.vector.tensor_copy(chunked(dec), spread(hs[:, HS_G, :])).then_inc(*ve_dn.step("gbc"))
                        for n, src, dst, th in (("k", ka, kT, Y), ("q", qa, qT, X), ("v", va, va, XT)):
                            ac(f"th{n}")
                            stt(out=dst[:, :], in0=th[:, :], scalar=1.0, in1=src[:, :], op0=ALU.add, op1=ALU.mult).then_inc(*ve_dn.step(f"{n}T"))
                        pe_("gr")
                        for c in range(NC):
                            a = ts(dec[:, c * P:c * P + P], bank[0][:, c * P:c * P + P], hs[:, HS_GC, c:c + 1], 0.0, ALU.subtract, ALU.min)
                        a.then_inc(*ve_dn.step("dmin"))
                        fill(2)
                        pe_("sk")
                        ts(sm[:, 0, :], bank[5][:, 0:NC], EPS, None, ALU.add).then_inc(*ve_dn.step("skE"))
                        me("skE")
                        nc.vector.reciprocal(sm[:, 1, :], sm[:, 0, :]).then_inc(*ve_dn.step("rden"))
                        me("rden")
                        tt(sm[:, 2, :], sm[:, 1, :], hs[:, HS_BETA, :], ALU.mult).then_inc(*ve_dn.step("bnk2"))
                        fill(1)
                        me("bnk2")
                        po_("decs")
                        pe_("kk")
                        for c in range(NC):
                            t = slice(c * P, c * P + P)
                            a = stt(out=NT[:, t], in0=bank[2][:, t], scalar=sm[:, 2, c:c + 1], in1=decs[:, t], op0=ALU.mult, op1=ALU.mult)
                        a.then_inc(*ve_dn.step("NT"))
                        me("NT")
                        tt(chunked(XT), chunked(NT), each_chunk(I_M1T), ALU.mult).then_inc(*ve_dn.step("m1"))
                        me("m1")
                        tt(chunked(XT), each_chunk(I_ID), chunked(XT), ALU.subtract).then_inc(*ve_dn.step("x2T"))
                        pe_("kq")
                        po_("deci")
                        tt(attn[:, :], attn[:, :], bank[3][:, :], ALU.mult).then_inc(*ve_dn.step("attnT"))
                        fill(1)
                    conv(0)
                    if dn:
                        level(0)
                        level(1)
                    conv(1)
                    if dn:
                        level(2)
                        level(3)
                    conv(2)
                    if dn:
                        level(4)
                        level(5)
                    if dense:
                        dve.wait_ge(ac_ds.sem, ac_ds.after(rd, "g_th"))
                        dve.wait_ge(ac_dn.sem, ac_dn.after(rd - 1, "sgc"))
                        stt(out=sgn[:, :], in0=gth[:, :], scalar=1.0, in1=bank[7][:, :], op0=ALU.add, op1=ALU.mult).then_inc(*ve_ds.step("sg"))
                    if dn:
                        for c in range(NC):
                            t = slice(c * P, c * P + P)
                            if c:
                                pe_(f"p{c}")
                                stt(out=R[:, :], in0=bank[0][:, 0:P], scalar=hs[:, HS_NEG, c:c + 1], in1=vs[:, t],
                                    op0=ALU.mult, op1=ALU.add).then_inc(*ve_dn.step(f"r{c}"))
                                fill(1)
                            pe_(f"vn{c}")
                            ts(VN[:, :], bank[1][:, 0:P], sm[:, 2, c:c + 1], None, ALU.mult).then_inc(*ve_dn.step(f"vn{c}"))
                            fill(1)
                            if c < NC - 1:
                                pe_(f"os{c}")
                                if c == 0:
                                    ts(S[:, :], bank[2][:, 0:P], 1.0, None, ALU.mult).then_inc(*ve_dn.step("s0"))
                                else:
                                    me(f"s{c - 1}")
                                    stt(out=S[:, :], in0=S[:, :], scalar=hs[:, HS_GL, c:c + 1], in1=bank[2][:, 0:P],
                                        op0=ALU.mult, op1=ALU.add).then_inc(*ve_dn.step(f"s{c}"))
                                fill(1)
                        ac("osq")
                        stt(out=og[:, :], in0=bank[4][:, :], scalar=hnh[:, 0:1], in1=sgc[:, :], op0=ALU.mult, op1=ALU.mult).then_inc(*ve_dn.step("og"))
                        pe_("so")
                        ts(sm[:, 4, :], bank[5][:, 0:NC], P * EPS * EPS, None, ALU.add).then_inc(*ve_dn.step("vE"))
                        fill(TAPS)
                    if dense:
                        dve.wait_ge(ac_ds.sem, ac_ds.after(rd, "gt_th"))
                        dve.wait_ge(taps, rd * TAPS + TAPS)
                        stt(out=c_raw[:, TAPS - 1:], in0=gth[:, :], scalar=1.0, in1=valb[:, :], op0=ALU.add, op1=ALU.mult).then_inc(*ve_ds.step("craw"))
                    if dn:
                        po_("rs")
                        nc.vector.tensor_copy(chunked(decs), spread(sm[:, 5, :])).then_inc(*ve_dn.step("fbc"))
                        me("og")
                        pe_("fb")
                        tt(og[:, :], og[:, :], bank[3][:, :], ALU.mult).then_inc(*ve_dn.step("oF"))
                        me("oF")
                        ts(o_hi[:, hn, :], og[:, :], 1.0, None, ALU.mult).then_inc(*ve_dn.step("ohi"))
                        me("ohi")
                        tt(o_lo[:, hn, :], og[:, :], o_hi[:, hn, :].bitcast(F32), ALU.subtract).then_inc(*ve_dn.step("olo"))

                dve.wait_ge(wab_in, l * 64 + 64)
                ts(hnh[:, :], hnw[:, :], 0.5, None, ALU.mult).then_inc(hn_done, 1)
                dve.wait_ge(hn_done, l + 1)
                Rh = l * R_LAYER + R_H
                head((Rh, 0, l * 8, 0), None, None)
                ab_sums()
                with dve.Fori(0, 3) as p:
                    for half in range(2):
                        head((Rh + p * 3, 6 + 6 * half, l * 8 + p * 2 + (1 + half), p * 2 + (1 + half)), p * 2 + half, l * 8 + p * 2 + half)
                head((Rh + 9, 6, l * 8 + 7, 7), 6, l * 8 + 6)
                for c in range(SLOTS):
                    lo(l * R_LAYER + R_T, None, c)
                head(None, 7, l * 8 + 7)

                norm_factor(None, l * 4 + 2)
                norm_fbc(l * 4 + 2)
                dve.wait_ge(bc, l * 4 + 3)
                for k in range(KT + 1):
                    if k < KT:
                        if k >= 2:
                            dve.wait_ge(clo_done, l * 8 + (k - 1))
                        stt(out=hf[k % 2][:, :], in0=c_all[:, k, :], scalar=pcol[:, k, PR_CN:PR_CN + 1], in1=bank[7][:, :],
                            op0=ALU.mult, op1=ALU.mult).then_inc(cn_done, 1)
                    if k:
                        b = (k - 1) % 2
                        dve.wait_ge(cth_done, l * 8 + k)
                        stt(out=hf[b][:, :], in0=cth[b][:, :], scalar=1.0, in1=hf[b][:, :], op0=ALU.add, op1=ALU.mult).then_inc(cp_done, 1)

                with dve.Fori(0, KT) as m:
                    Rd = l * R_LAYER + m + R_T
                    n = l * 16 + m * 2
                    for c in range(4):
                        if c >= 2:
                            dve.wait_ge(used, Rd * 4 + (c + 1 + SLOTS))
                            dve.wait_ge(mg_done, l * 8 + m + 1)
                            dve.wait_ge(th_done, n + (c - 2 + 1 + 2))
                            stt(out=(t0, t1)[c - 2][:, :], in0=(thA, thB)[c - 2][:, :], scalar=1.0, in1=bank[c][:, :],
                                op0=ALU.add, op1=ALU.mult).then_inc(ta_done, 1)
                        if c == 3:
                            dve.wait_ge(ta_done, n + 4)
                            tt(mg[:, m, :], t0[:, :], t1[:, :], ALU.add).then_inc(mg_done, 1)
                        lo(Rd, None, c + 4)
                for i in range(2):
                    for c in range(4):
                        lo(l * R_LAYER + (R_O + i), None, c + 4)
                        add_x(4 * i + c, l * R_LAYER + (R_O + i), c, None, 0.5, 4 + c % 2)
                ffn(l, 1, R_F2, V_F2, R_D2, V_D2, 2, l * 4 + 3, PR_F2)

            norm_factor(None, 4 * DEPTH)
            dve.wait_ge(rs_done, 4 * DEPTH + 1)
            dve.wait_ge(par_in, DEPTH * 160 + 16)
            for c in range(NC):
                for half in range(2):
                    n = 2 * c + half
                    dve.wait_ge(fin_t, n + 1)
                    cols = slice(half * 512, half * 512 + 512)
                    stt(out=raw[c][:, cols], in0=bank[n % 2][:, :], scalar=nrm[:, 1, c:c + 1], in1=prow[:, cols],
                        op0=ALU.mult, op1=ALU.mult).then_inc(fin_y, 1)

        @block.gpsimd
        def _(pool):
            tt = nc.gpsimd.tensor_tensor
            for s_, n_ in ((lo_v, SLOTS), (lo_g, SLOTS), (used, SLOTS), (silu_done, 2), (prod_done, 2), (th_done, 2), (ta_done, 2),
                           (par_t, 1), (taps, TAPS), (mg_done, 1)):
                pool.sem_inc(s_, n_)
            for st in (pe_dn, ve_dn, ac_dn, po_dn, ac_ds, ve_ds):
                pool.sem_inc(st.sem, len(st.names))

            def lo(Rd, c):
                pool.wait_ge(hi_done, Rd * 4 + (c + 1))
                tt(w_lo[c % SLOTS][:, :], raw[c % SLOTS][:, :], w_hi[c % SLOTS][:, :].bitcast(F32), ALU.subtract).then_inc(lo_g, 1)

            def sum_squares(done, sums, n, base):
                for m in range(1, n + 1):
                    pool.wait_ge(done, base * 8 + (m + 1))
                    if m > 1:
                        pool.wait_ge(sums, base * n + (m - 1))
                    tt(ssq[:, :], ssq[:, :], sqb[m % 2][:, :], ALU.add).then_inc(sums, 1)

            def inverse_root(nf):
                pool.wait_ge(var_done, nf + 1)
                tt(nrm[:, 1, :], nrm[:, 0, :], pw[:, 0, :], ALU.pow).then_inc(rs_done, 1)

            def h_rest(nh):
                for k in range(0, KT, 2):
                    pool.wait_ge(hhi_done, nh * 8 + (k + 1))
                    tt(h_lo[:, k, :], hb[k % 4][:, :], h_hi[:, k, :].bitcast(F32), ALU.subtract).then_inc(hlo_g, 1)

            def norm(nh, nf):
                inverse_root(nf)
                h_rest(nh)

            pool.wait_ge(init, 4)
            sum_squares(sq_done, ssq_done, KT - 2, 0)
            with pool.Fori(0, DEPTH) as l:
                norm(l * 3, l * 4)
                sum_squares(sq_done, ssq_done, KT - 2, l * 3 + 1)
                Rh = l * R_LAYER + R_H
                norm(l * 3 + 1, l * 4 + 1)
                for c in range(SLOTS):
                    lo(Rh, c)

                def head(dense, rn):
                    def step(name):
                        if rn is None:
                            return
                        if name == "decs":
                            pool.wait_ge(ac_dn.sem, ac_dn.after(rn, "decT"))
                            tt(chunked(decs), chunked(dec), each_chunk(I_STRICT), ALU.mult).then_inc(*po_dn.step("decs"))
                        elif name == "rk":
                            pool.wait_ge(ve_dn.sem, ve_dn.after(rn, "skE"))
                            tt(sm[:, 3, :], sm[:, 0, :], pw[:, 1, :], ALU.pow).then_inc(*po_dn.step("rk"))
                        elif name == "deci":
                            tt(chunked(attn), chunked(dec), each_chunk(I_INCL), ALU.mult).then_inc(*po_dn.step("deci"))
                        elif name == "qd":
                            pool.wait_ge(ac_dn.sem, ac_dn.after(rn, "eg"))
                            pool.wait_ge(ve_dn.sem, ve_dn.after(rn, "qT"))
                            tt(qd[:, :], qd[:, :], qT[:, :], ALU.mult).then_inc(*po_dn.step("qd"))
                        else:
                            pool.wait_ge(ve_dn.sem, ve_dn.after(rn, "vE"))
                            tt(sm[:, 5, :], sm[:, 4, :], pw[:, 0, :], ALU.pow).then_inc(*po_dn.step("rs"))

                    step("decs")
                    step("rk")
                    for t in range(6):
                        if dense and t < dense[2]:
                            lo(dense[0], dense[1] + t + 4)
                        if t == 0:
                            step("deci")
                            step("qd")
                    step("rs")

                head((Rh, 0, 6), None)
                with pool.Fori(0, 3) as p:
                    for half in range(2):
                        head((Rh + p * 3, 6 + 6 * half, 6), l * 8 + p * 2 + half)
                head((Rh + 9, 6, 2), l * 8 + 6)
                head(None, l * 8 + 7)
                sum_squares(cf_done, csq_done, KT - 1, l)
                inverse_root(l * 4 + 2)
                for k in range(KT):
                    pool.wait_ge(chi_done, l * 8 + (k + 1))
                    tt(c_lo[:, k, :], hf[k % 2][:, :], c_hi[:, k, :].bitcast(F32), ALU.subtract).then_inc(clo_done, 1)
                for k in range(KT):
                    pool.wait_ge(mghi_done, l * 8 + (k + 1))
                    tt(mg_lo[:, k, :], mg[:, k, :], mg_hi[:, k, :].bitcast(F32), ALU.subtract).then_inc(mglo_done, 1)
                sum_squares(sq_done, ssq_done, KT - 2, l * 3 + 2)
                norm(l * 3 + 2, l * 4 + 3)
                sum_squares(sq_done, ssq_done, KT - 2, l * 3 + 3)
            inverse_root(4 * DEPTH)


_INS = ["x", "ffn1_norm", "ffn1_w_gate", "ffn1_w_up", "ffn1_w_down", "mix_norm", "w_in", "qkv_conv_w", "a_log",
        "dt_bias", "head_norm", "w_a_out", "dw_conv_w", "dw_conv_b", "conv_norm", "w_b_out", "w_o", "ffn2_norm",
        "ffn2_w_gate", "ffn2_w_up", "ffn2_w_down", "final_norm"]


def kernel(**inputs):
    import concourse.bacc as _bacc
    from concourse.bass_utils import run_bass_kernel_spmd as _run

    nc = _bacc.Bacc("TRN2", target_bir_lowering=False, num_devices=1)
    arrays, args = {}, []
    for name in _INS + ["consts"]:
        a = constants() if name == "consts" else np.ascontiguousarray(inputs[name])
        arrays[f"in_{name}"] = a
        args.append(nc.dram_tensor(f"in_{name}", a.shape, mybir.dt.from_np(a.dtype), kind="ExternalInput").ap())
    out = nc.dram_tensor("out_x", (1, SEQ, D), F32, kind="ExternalOutput").ap()
    trunk(nc, *args, out)
    return _run(nc, [arrays], core_ids=[0]).results[0]["out_x"]
```

```python
from contextlib import ExitStack

import numpy as np

import concourse.bass as bass
from concourse import mybir
from concourse.alu_op_type import AluOpType as ALU

P = 128
DEPTH, SEQ, D, FF, HEADS = 2, 512, 1024, 2816, 8
KT = D // P
FT = FF // P
NC = SEQ // P
TAPS, SC = 31, 4
EPS = 1e-6
SLOTS = 4
UNIT = KT * P
DSPLIT = [(0, 8), (8, 16), (16, 22)]
F32, F32R = mybir.dt.float32, mybir.dt.float32r
ACT = mybir.ActivationFunctionType

R_F1, R_D1, R_H, R_T, R_O, R_F2, R_D2, R_LAYER = 0, 11, 17, 29, 37, 39, 50, 56
V_F1, V_D1, V_T, V_O, V_F2, V_D2, V_LAYER = 0, 11, 17, 23, 25, 36, 42
G_LAYER = 14
PRE = 3

C_Q, C_K, C_V, C_G, C_AB, C_VAL, C_GT, C_GA, C_GB = 0, D, 2 * D, 3 * D, 4 * D, 4 * D + 16, 5 * D + 16, 6 * D + 16, 7 * D + 16

PR_DW, PR_B, PR_CN, PR_F1, PR_MIX, PR_F2, PR_QKV, PR_N = 0, 31, 32, 33, 34, 35, 36, 48

I_ID, I_INCL, I_STRICT, I_M1T, I_LV = 0, 1, 2, 3, 4
LEVELS = 6

AB_V, AB_G = 15, 13

HS_G, HS_GC, HS_NEG, HS_BETA, HS_KD, HS_GL, HS_N = 0, 1, 2, 3, 4, 5, 6


def constants():
    r, c = np.arange(P)[:, None], np.arange(P)[None, :]
    mats = [r == c, r <= c, r < c, (r % 2 == 0) & (c == r + 1)]
    for lv in range(LEVELS):
        s = 2 << lv
        mats.append(((r // s) % 2 == 1) & (c // s == r // s - 1))
    return np.ascontiguousarray(np.stack(mats, 1).astype(np.float32))


class Steps:

    def __init__(self, sem, names):
        self.sem, self.names, self.at, self.n = sem, names, {x: i + 1 for i, x in enumerate(names)}, 0
        assert len(self.at) == len(names)

    def step(self, name):
        assert self.names[self.n % len(self.names)] == name, (name, self.names[self.n % len(self.names)])
        self.n += 1
        return self.sem, 1

    def after(self, rnd, name):
        return (rnd + 1) * len(self.names) + self.at[name]


PE_ORDER = "H H H gr H H kt H so kk H H kq vt H H fb H H H H x2t H H y0 H H H H xy0 xt0".split()
for _l in range(1, LEVELS - 1):
    PE_ORDER += f"{'H H' if _l == 1 else 'H H H'} y{_l} H H H H xy{_l} xt{_l}".split()
PE_ORDER += f"H H H y{LEVELS - 1} H H H xy{LEVELS - 1} H H vn0 H H os0".split()
for _c in range(1, NC):
    PE_ORDER += f"H H p{_c} H vn{_c} H H os{_c}".split()
HALVES = 12
assert PE_ORDER.count("H") == 6 * HALVES, PE_ORDER.count("H")
PE_STEPS = [x for x in PE_ORDER if x not in ("H", "so", "fb")]
PE_TAIL = ["so", "fb"]

DVE_STEPS = ["hs", "gbc", "kT", "qT", "vT", "dmin", "skE", "rden", "bnk2", "NT", "m1", "x2T", "attnT"]
for _l in range(LEVELS):
    DVE_STEPS += [f"y{_l}", f"x{_l}"] + ([f"xt{_l}"] if _l < LEVELS - 1 else [])
DVE_STEPS += ["vn0", "s0"]
for _c in range(1, NC):
    DVE_STEPS += [f"r{_c}", f"vn{_c}"] + ([f"s{_c}"] if _c < NC - 1 else [])
DVE_TAIL = ["og", "vE", "fbc", "oF", "ohi", "olo"]

ACT_STEPS = ["thk", "thq", "thv", "sgc", "ksq", "decT", "eg", "kd", "X2", "vs", "qsq"]
POOL_STEPS = ["decs", "deci", "rk", "qd"]
ACT_DENSE = ["q_raw", "q_tap", "k_raw", "k_tap", "v_raw", "v_tap", "g_th", "val", "gt_th"]
DVE_DENSE = ["dcol", "q1", "q2", "q3", "k1", "k2", "k3", "v1", "v2", "v3", "sg", "craw"]


def trunk(nc, x, ffn1_norm, ffn1_w_gate, ffn1_w_up, ffn1_w_down, mix_norm, w_in, qkv_conv_w, a_log,
          dt_bias, head_norm, w_a_out, dw_conv_w, dw_conv_b, conv_norm, w_b_out, w_o, ffn2_norm,
          ffn2_w_gate, ffn2_w_up, ffn2_w_down, final_norm, consts, out):
    ds = bass.ds
    with ExitStack() as ctx:
        place = [(nc.sbuf_base + 31) // 32 * 32]

        def sb(name, shape, dt=F32):
            t = nc.alloc_sbuf_tensor_at(name, [P, *shape], dt, offset=place[0])
            place[0] += (4 * int(np.prod(shape)) + 31) // 32 * 32
            return t

        cst = sb("cst", [I_LV + LEVELS, P])
        ident = cst[:, I_ID, :]
        incl = cst[:, I_INCL, :]
        ones = sb("ones", [P])
        xT = sb("xT", [KT, SEQ])
        h_hi = sb("h_hi", [KT, SEQ], F32R)
        h_lo = sb("h_lo", [KT, SEQ], F32R)
        raw = [sb(f"raw{s}", [UNIT]) for s in range(SLOTS)]
        w_hi = [sb(f"w_hi{s}", [UNIT], F32R) for s in range(SLOTS)]
        w_lo = [sb(f"w_lo{s}", [UNIT], F32R) for s in range(SLOTS)]
        row_at = place[0]
        prow = sb("prow", [D])
        pcol = sb("pcol", [KT, PR_N])
        ssq = sb("ssq", [SEQ])
        sqb = [sb(f"sqb{i}", [SEQ]) for i in range(2)]
        nrm = sb("nrm", [4, NC])
        pw = sb("pw", [2, NC])
        fbc = sb("fbc", [NC, P])
        hf = [sb(f"hf{i}", [SEQ]) for i in range(2)]
        hnw = sb("hnw", [1])
        hnh = sb("hnh", [1])
        hb = [*hf, *sqb]
        arena = place[0]

        x_sq = sb("x_sq", [KT, SEQ])
        place[0] = arena

        act_hi = sb("act_hi", [FT, SEQ], F32R)
        act_lo = sb("act_lo", [FT, SEQ], F32R)
        sg_f, a_f = hf, sqb
        ffn_end = place[0]

        place[0] = arena
        o_hi = sb("o_hi", [HEADS, SEQ], F32R)
        o_lo = sb("o_lo", [HEADS, SEQ], F32R)
        c_at = place[0]
        c_all = sb("c_all", [KT, SEQ])
        dn_at = place[0]
        q_raw = sb("q_raw", [SEQ + SC - 1])
        k_raw = sb("k_raw", [SEQ + SC - 1])
        v_raw = sb("v_raw", [SEQ + SC - 1])
        qa, ka, va = (sb(n, [SEQ]) for n in ("qa", "ka", "va"))
        assert place[0] - dn_at >= 2 * PRE * SEQ * 4
        c_raw = sb("c_raw", [SEQ + TAPS - 1])
        cacc = sb("cacc", [SEQ])
        delta_at = place[0]
        (qT, kT, dec, decs, attn, qd, NT, X, XT, Y) = (
            sb(n, [SEQ]) for n in "qT kT dec decs attn qd NT X XT Y".split())
        valb, gth, sgn, sgc, og = hf[0], hf[1], sqb[0], sqb[1], ssq
        S, R, VN = (sb(n, [P]) for n in ("S", "R", "VN"))
        hsc = sb("hsc", [HEADS, HS_N, NC])
        hs = sb("hs", [HS_N, NC])
        sm = sb("sm", [6, NC])
        ksum = sb("ksum", [NC])
        ncol = sb("ncol", [PR_N])
        dcol = sb("dcol", [PR_N])
        dn_end = place[0]
        place[0] = c_at
        ab = sb("ab", [NC, 16])
        abT = sb("abT", [SEQ])
        abw = sb("abw", [8, HEADS, NC])
        alb = sb("alb", [2, HEADS])
        wab_raw = sb("wab_raw", [KT, 16])
        wab_hi = sb("wab_hi", [KT, 16], F32R)
        wab_lo = sb("wab_lo", [KT, 16], F32R)
        place[0] = row_at
        kd = sb("kd", [SEQ])
        vs = sb("vs", [SEQ])
        place[0] = dn_at
        mg = sb("mg", [KT, SEQ])
        assert place[0] <= delta_at
        place[0] = delta_at
        c_lo = sb("c_lo", [KT, SEQ], F32R)
        cth = [sb(f"cth{i}", [SEQ]) for i in range(2)]
        assert max(place[0], ffn_end, dn_end) <= nc.sbuf_usable_end, (place[0], ffn_end, dn_end, nc.sbuf_usable_end)
        place[0] = c_at
        c_hi = sb("c_hi", [KT, SEQ], F32R)
        place[0] = arena
        mg_hi = sb("mg_hi", [KT, SEQ], F32R)
        mg_lo = sb("mg_lo", [KT, SEQ], F32R)
        thA, thB, t0, t1 = hf[0], hf[1], sqb[0], sqb[1]
        csum, csq = hf[1], (hf[0], sqb[0])

        bank = [ctx.enter_context(nc.psum_tensor(f"bank{i}", [P, SEQ], F32)) for i in range(8)]

        def sem(name):
            return ctx.enter_context(nc.semaphore(name))

        const_in = sem("const_in")
        ident_in = sem("ident_in")
        x_in = [sem(f"x_in{k}") for k in range(NC)]
        init = sem("init")
        raw_landed = [sem(f"raw_landed{s}") for s in range(SLOTS)]
        hi_done = sem("hi_done")
        lo_v = sem("lo_v")
        lo_g = sem("lo_g")
        used = sem("used")
        xt_done = sem("xt_done")
        x_upd = sem("x_upd")
        sq_done = sem("sq_done")
        ssq_done = sem("ssq_done")
        stat = sem("stat")
        var_done = sem("var_done")
        rs_done = sem("rs_done")
        fbc_done = sem("fbc_done")
        bc = sem("bc")
        hf_done = sem("hf_done")
        hhi_done = sem("hhi_done")
        hlo_g = sem("hlo_g")
        hlo_v = sem("hlo_v")
        silu_done = sem("silu_done")
        gs_done = sem("gs_done")
        ub_done = sem("ub_done")
        hx_done = sem("hx_done")
        rinv_done = sem("rinv_done")
        prod_done = sem("prod_done")
        acthi_done = sem("acthi_done")
        actlo_done = sem("actlo_done")
        par_in = sem("par_in")
        par_t = sem("par_t")
        par_done = sem("par_done")
        par_norm = sem("par_norm")
        wab_in = sem("wab_in")
        abhi_done = sem("abhi_done")
        ablo_done = sem("ablo_done")
        ab_pe = sem("ab_pe")
        ab_v = sem("ab_v")
        ab_a = sem("ab_a")
        taps = sem("taps")
        csq_done = sem("csq_done")
        cf_done = sem("cf_done")
        cth_done = sem("cth_done")
        cn_done = sem("cn_done")
        cp_done = sem("cp_done")
        ab_h = sem("ab_h")
        hn_done = sem("hn_done")
        chi_done = sem("chi_done")
        clo_g = sem("clo_g")
        clo_v = sem("clo_v")
        gate_done = sem("gate_done")
        t_done = sem("t_done")
        th_done = sem("th_done")
        ta_done = sem("ta_done")
        mg_done = sem("mg_done")
        mghi_done = sem("mghi_done")
        mglo_g = sem("mglo_g")
        mglo_v = sem("mglo_v")
        fin_t = sem("fin_t")
        fin_y = sem("fin_y")
        stored = sem("stored")
        pe_dn = Steps(sem("pe_dn"), PE_STEPS)
        ve_dn = Steps(sem("ve_dn"), DVE_STEPS)
        ac_dn = Steps(sem("ac_dn"), ACT_STEPS)
        po_dn = Steps(sem("po_dn"), POOL_STEPS)
        pe_tl = Steps(sem("pe_tl"), PE_TAIL)
        ve_tl = Steps(sem("ve_tl"), DVE_TAIL)
        ac_tl = Steps(sem("ac_tl"), ["osq"])
        po_tl = Steps(sem("po_tl"), ["sum", "rs"])
        ac_ds = Steps(sem("ac_ds"), ACT_DENSE)
        ve_ds = Steps(sem("ve_ds"), DVE_DENSE)

        block = ctx.enter_context(nc.Block())
        X_TILES = 8 + 24 * DEPTH

        def chunked(t):
            return t[:, :].rearrange("p (c i) -> p c i", c=NC)

        def each_chunk(i):
            return cst[:, i:i + 1, :].broadcast_to([P, NC, P])

        def spread(cols):
            return cols.rearrange("p (c o) -> p c o", o=1).broadcast_to([P, NC, P])

        @block.sync
        def _(sp):
            sp.dma_start(cst[:, 0:1, :], consts[:, 0:1, :]).then_inc(ident_in, 16)
            for k in range(NC):
                sp.dma_start(raw[k][:, :], x[0, k * P:(k + 1) * P, :]).then_inc(x_in[k], 16)
            w_in_v = w_in.rearrange("l (k p) c -> l p k c", p=P)

            def unit(Rd, own, mine, c, src, kts=KT):
                if mine is not None:
                    sp.wait_ge(mine, own * 4 + (c + 1))
                dst = raw[c % SLOTS][:, 0:kts * P].rearrange("p (k c) -> p k c", k=kts)
                sp.dma_start(dst, src).then_inc(raw_landed[c % SLOTS], 16)

            def ffn_units(l, w_gate, w_up, w_down, r_f, v_f, r_d, v_d):
                wg, wu, wd = (w.rearrange("l (k p) c -> l p k c", p=P) for w in (w_gate, w_up, w_down))
                with sp.Fori(0, FT // 2) as i:
                    for c in range(4):
                        src = (wg, wu)[c % 2][l, :, :, ds(i * 256 + (c // 2) * P, P)]
                        unit(l * R_LAYER + i + r_f, l * V_LAYER + i + v_f, lo_v, c, src)
                with sp.Fori(0, 2) as i:
                    for c in range(12):
                        a, b = DSPLIT[c % 3]
                        src = wd[l, :, a:b, ds(i * 512 + (c // 3) * P, P)]
                        unit(l * R_LAYER + i * 3 + r_d, l * V_LAYER + i * 3 + v_d, lo_v, c, src, b - a)

            sp.wait_ge(init, 4)
            sp.dma_start(cst[:, 1:, :], consts[:, 1:, :]).then_inc(const_in, 16)
            with sp.Fori(0, DEPTH) as l:
                sp.wait_ge(par_t, l + 1)
                sp.dma_start(prow[PR_DW:PR_DW + TAPS, :], dw_conv_w[l]).then_inc(par_in, 16)
                for row, v in ((PR_B, dw_conv_b), (PR_CN, conv_norm), (PR_F1, ffn1_norm), (PR_MIX, mix_norm), (PR_F2, ffn2_norm)):
                    sp.dma_start(prow[row:row + 1, :], v[ds(l, 1), :]).then_inc(par_in, 16)
                for t in range(SC):
                    sp.dma_start(prow[PR_QKV + 3 * t:PR_QKV + 3 * t + 3, :],
                                 qkv_conv_w[l, t].rearrange("(q c) -> q c", q=3)).then_inc(par_in, 16)
                sp.wait_ge(xt_done, NC)
                ffn_units(l, ffn1_w_gate, ffn1_w_up, ffn1_w_down, R_F1, V_F1, R_D1, V_D1)
                sp.wait_ge(lo_v, l * (V_LAYER * 4) + (V_T * 4 + SLOTS))
                head_cols = (C_Q, C_K, C_V, C_G, C_VAL, C_GT)

                def head_units(hd, Rd, G, c0, ts=range(6), every=False):
                    for t in ts:
                        unit(Rd, G, lo_g if every or c0 + t >= SLOTS else None, c0 + t, w_in_v[l, :, :, ds(hd * P + head_cols[t], P)])

                head_units(0, l * R_LAYER + R_H, l * G_LAYER, 0, range(SLOTS))
                sp.wait_ge(x_upd, l * 24 + 16)
                sp.dma_start(wab_raw[:, :, :], w_in_v[l, :, :, C_AB:C_AB + 16]).then_inc(wab_in, 16)
                sp.dma_start(alb[:, 0, :], a_log[ds(l, 1), :].broadcast_to([P, HEADS])).then_inc(wab_in, 16)
                sp.dma_start(alb[:, 1, :], dt_bias[ds(l, 1), :].broadcast_to([P, HEADS])).then_inc(wab_in, 16)
                sp.dma_start(hnw[:, :], head_norm[l].rearrange("(p o) -> p o", o=1)).then_inc(wab_in, 16)
                head_units(0, l * R_LAYER + R_H, l * G_LAYER, 0, range(SLOTS, 6))
                head_units(1, l * R_LAYER + R_H, l * G_LAYER, 6)
                with sp.Fori(0, 3) as p:
                    for half in range(2):
                        head_units(p * 2 + (2 + half), l * R_LAYER + p * 3 + (R_H + 3), l * G_LAYER + p * 3 + 3, 6 * half, every=True)
                wa, wb, wo = (w.rearrange("l (k p) c -> l p k c", p=P) for w in (w_a_out, w_b_out, w_o))

                def gate(c_gate, m):
                    return w_in_v[l, :, :, ds(m * P + c_gate, P)]

                first = [gate(cg, m) for m in range(PRE) for cg in (C_GA, C_GB)]
                first += [w[l, :, :, m * P:m * P + P] for w in (wa, wb) for m in range(PRE)]
                for c, src in enumerate(first):
                    if c < 12:
                        unit(l * R_LAYER + R_T, l * G_LAYER + 12, lo_g, c, src)
                with sp.Fori(0, KT - PRE) as i:
                    for c in range(4):
                        src = gate((C_GA, C_GB)[c], i + PRE) if c < 2 else (wa, wb)[c - 2][l, :, :, ds(i * P + PRE * P, P)]
                        unit(l * R_LAYER + i + (R_T + 3), l * V_LAYER + i + (V_T + 1), lo_v, c, src)
                with sp.Fori(0, 2) as i:
                    for c in range(4):
                        unit(l * R_LAYER + i + R_O, l * V_LAYER + i + V_O, lo_v, c, wo[l, :, :, ds(i * 512 + c * P, P)])
                ffn_units(l, ffn2_w_gate, ffn2_w_up, ffn2_w_down, R_F2, V_F2, R_D2, V_D2)
            sp.wait_ge(par_t, DEPTH + 1)
            sp.dma_start(prow[:, :], final_norm.rearrange("(o c) -> o c", o=1).broadcast_to([P, D])).then_inc(par_in, 16)
            for c in range(NC):
                for half in range(2):
                    sp.wait_ge(fin_y, 2 * c + half + 1)
                    sp.dma_start(out[0, c * P:(c + 1) * P, half * 512:half * 512 + 512],
                                 raw[c][:, half * 512:half * 512 + 512]).then_inc(stored, 16)
            sp.wait_ge(stored, 16 * 2 * NC)

        @block.tensor
        def _(pe):
            def mm(o, a, b, start=True, stop=True, **kw):
                return nc.tensor.matmul(o, a, b, start=start, stop=stop, **kw)

            def three(bk, slot, kk, a_hi, a_lo, k, first, last, only=None):
                w = slice(kk * P, kk * P + P)
                r = None
                for j, (wt, at) in enumerate(((w_hi, a_hi), (w_hi, a_lo), (w_lo, a_hi))):
                    if only is None or only == j:
                        r = mm(bank[bk][:, :], wt[slot][:, w], at[:, k, :], start=first and j == 0, stop=last and j == 2)
                return r

            def norm_stats(rn):
                pe.wait_ge(ssq_done, rn * 7 + 7)
                for c in range(NC):
                    m = mm(bank[6][:, c:c + 1], ssq[:, c * P:c * P + P], ones[:, 0:1])
                m.then_inc(stat, 1)

            def norm_spread(nf):
                pe.wait_ge(fbc_done, nf + 1)
                for c in range(NC):
                    m = mm(bank[7][:, c * P:c * P + P], fbc[:, c, :], ident)
                m.then_inc(bc, 1)

            def ffn(l, w, r_f, v_f, r_d, v_d, nrm_i, nf, base_upd):
                def unit(i, c, first=False):
                    pe.wait_ge(lo_v, l * (V_LAYER * 4) + i * 4 + (v_f * 4 + c + 1 + SLOTS))
                    pe.wait_ge((gs_done, ub_done)[c % 2], l * (2 * FT) + i * 2 + (w * FT + c // 2 + 1))
                    for k in range(KT):
                        if first:
                            pe.wait_ge(hx_done, l * 16 + (w * 8 + k + 1))
                        m = three(c, c, k, h_hi, h_lo, k, k == 0, k == KT - 1)
                    m.then_inc(used, 1)

                for c in range(4):
                    unit(0, c, c == 0)
                    if c == 1:
                        norm_stats(l * 3 + nrm_i)
                    if c == 2:
                        norm_spread(nf)
                with pe.Fori(0, FT // 2 - 1) as i:
                    for c in range(4):
                        unit(i + 1, c)
                with pe.Fori(0, 2) as i:
                    for j in range(4):
                        pe.wait_ge(x_upd, l * 24 + i * 4 + (base_upd + j - 1))
                        for q in range(3):
                            c = 3 * j + q
                            pe.wait_ge(lo_v, l * (V_LAYER * 4) + i * 12 + (v_d * 4 + c + 1 + SLOTS))
                            a, b = DSPLIT[q]
                            for k in range(a, b):
                                if j == 0:
                                    pe.wait_ge(actlo_done, l * (2 * FT) + (w * FT + k + 1))
                                m = three(4 + j % 2, c % SLOTS, k - a, act_hi, act_lo, k, k == 0, k == FT - 1)
                            m.then_inc(used, 1)

            pe.wait_ge(ident_in, 16)
            pe.wait_ge(init, 4)
            for c in range(NC):
                pe.wait_ge(x_in[c], 16)
                for k in range(KT):
                    m = nc.tensor.transpose(bank[k][:, c * P:c * P + P], raw[c][:, k * P:k * P + P], ident)
                m.then_inc(xt_done, 1)

            with pe.Fori(0, DEPTH) as l:
                pe.wait_ge(par_in, l * 160 + 160)
                pe.wait_ge(x_upd, l * 24 + 2)
                for k in range(KT):
                    m = nc.tensor.transpose(bank[k // 4][:, k % 4 * P:k % 4 * P + P], prow[:, k * P:k * P + P], ident)
                m.then_inc(par_t, 1)
                ffn(l, 0, R_F1, V_F1, R_D1, V_D1, 0, l * 4, 8)

                norm_stats(l * 3 + 1)
                norm_spread(l * 4 + 1)
                pe.wait_ge(ablo_done, l + 1)
                for k in range(KT):
                    pe.wait_ge((hlo_g, hlo_v)[k % 2], l * 4 + (k // 2 + 1))
                    for j, (wt, at) in enumerate(((wab_hi, h_hi), (wab_hi, h_lo), (wab_lo, h_hi))):
                        m = mm(bank[0][0:16, :], wt[:, k, :], at[:, k, :], start=(k == 0 and j == 0), stop=(k == KT - 1 and j == 2))
                m.then_inc(ab_pe, 1)

                def ab_turn():
                    pe.wait_ge(ab_v, l * AB_V + 1)
                    for c in range(NC):
                        m = mm(bank[1][:, c * 16:c * 16 + 16], abT[0:16, c * P:c * P + P], cst[0:16, I_ID, 0:16])
                    m.then_inc(ab_pe, 1)

                def ab_sums():
                    pe.wait_ge(const_in, 16)
                    pe.wait_ge(ab_v, l * AB_V + AB_G)
                    mm(bank[1][:, 0:32], incl, hsc[:, :, HS_G, :])
                    mm(bank[1][:, 32:64], ones[:, :], hsc[:, :, HS_G, :]).then_inc(ab_pe, 1)

                def dense_half(s, Rg, c0, rd):
                    t, part = divmod(s, HALVES)
                    slot = (c0 + t) % SLOTS
                    if part == 0:
                        pe.wait_ge(lo_g, Rg * 4 + (c0 + t + 1 + SLOTS))
                        if t < 2:
                            last = l * 8 + 7 if rd is None else rd - 1
                            pe.wait_ge(ac_ds.sem, ac_ds.after(last, ("val", "gt_th")[t]))
                        elif rd is None:
                            pe.wait_ge(gate_done, l * (2 * PRE) + (t - 1))
                        elif t < 5:
                            pe.wait_ge(ac_ds.sem, ac_ds.after(rd, ("q_tap", "k_tap", "v_tap")[t - 2]))
                        else:
                            pe.wait_ge(ve_ds.sem, ve_ds.after(rd, "sg"))
                    for n in range(2 * part, 2 * part + 2):
                        k, j = divmod(n, 3)
                        m = three(6 + t % 2, slot, k, h_hi, h_lo, k, k == 0, k == KT - 1, only=j)
                    if part == HALVES - 1:
                        m.then_inc(used, 1)

                def each(o, a, b, name):
                    for c in range(NC):
                        m = mm(o[:, c * P:c * P + P], a[:, c * P:c * P + P], b[:, c * P:c * P + P])
                    m.then_inc(*pe_dn.step(name))

                def turn(o, a, name):
                    for c in range(NC):
                        m = nc.tensor.transpose(o[:, c * P:c * P + P], a[:, c * P:c * P + P], ident)
                    m.then_inc(*pe_dn.step(name))

                def stage(name, rn):
                    def ve(n, r=rn):
                        pe.wait_ge(ve_dn.sem, ve_dn.after(r, n))

                    def ac(n, r=rn):
                        pe.wait_ge(ac_dn.sem, ac_dn.after(r, n))

                    if name == "gr":
                        ve("gbc")
                        for c in range(NC):
                            m = mm(bank[0][:, c * P:c * P + P], dec[:, c * P:c * P + P], incl)
                        m.then_inc(*pe_dn.step(name))
                    elif name == "kt":
                        ve("kT")
                        turn(bank[1], kT, name)
                    elif name == "kk":
                        each(bank[2], kT, kT, name)
                    elif name == "kq":
                        ve("qT")
                        each(bank[3], kT, qT, name)
                    elif name == "vt":
                        ve("vT")
                        pe.wait_ge(ve_tl.sem, ve_tl.after(rn - 1, "og"))
                        turn(bank[4], va, name)
                    elif name == "x2t":
                        ve("x2T")
                        ac("eg")
                        turn(bank[0], XT, name)
                    elif name[0] == "y":
                        lv = int(name[1:])
                        ac("X2")
                        ac("kd")
                        if lv:
                            ve(f"x{lv - 1}")
                        each(bank[1], NT, X, name)
                    elif name[:2] == "xy":
                        pass
                    elif name[:2] == "xt":
                        lv = int(name[2:])
                        ve("attnT")
                        if lv:
                            ve(f"xt{lv - 1}")
                        each(bank[3], Y, XT, name)
                    elif name[:2] == "vn":
                        c = int(name[2:])
                        ac("vs")
                        if c:
                            ve(f"r{c}")
                        else:
                            ve(f"x{LEVELS - 1}")
                        mm(bank[1][:, 0:P], XT[:, c * P:c * P + P], (R[:, :] if c else vs[:, 0:P])).then_inc(*pe_dn.step(name))
                    elif name[:2] == "os":
                        c = int(name[2:])
                        t = slice(c * P, c * P + P)
                        ve(f"vn{c}")
                        pe.wait_ge(po_dn.sem, po_dn.after(rn, "qd"))
                        if c:
                            mm(bank[4][:, t], S[:, :], qd[:, t], stop=False)
                        m = mm(bank[4][:, t], VN[:, :], attn[:, t], start=(c == 0))
                        if c < NC - 1:
                            m = mm(bank[2][:, 0:P], kd[:, t], VN[:, :])
                        m.then_inc(*pe_dn.step(name))
                    elif name[0] == "p":
                        c = int(name[1:])
                        ve(f"s{c - 1}")
                        mm(bank[0][:, 0:P], kT[:, c * P:c * P + P], S[:, :]).then_inc(*pe_dn.step(name))

                def tail(name, rn):
                    if name == "so":
                        pe.wait_ge(po_tl.sem, po_tl.after(rn, "sum"))
                        pe.wait_ge(ve_tl.sem, ve_tl.after(rn - 1, "oF"))
                        for c in range(NC):
                            m = mm(bank[5][:, c:c + 1], attn[:, c * P:c * P + P], ones[:, 0:1])
                    else:
                        pe.wait_ge(ve_tl.sem, ve_tl.after(rn, "fbc"))
                        for c in range(NC):
                            m = mm(bank[5][:, c * P:c * P + P], fbc[:, c, :], ident)
                    m.then_inc(*pe_tl.step(name))

                def xy(lv, rn):
                    pe.wait_ge(ve_dn.sem, ve_dn.after(rn, f"y{lv}"))
                    if lv < LEVELS - 1:
                        each(bank[2], XT, Y, f"xy{lv}")
                    else:
                        each(bank[2], Y, XT, f"xy{lv}")

                def run_stage(name, rn):
                    if name.startswith("xy"):
                        xy(int(name[2:]), rn)
                    else:
                        stage(name, rn)

                def head(dense, rn, before=True):
                    s = 0
                    for name in PE_ORDER:
                        if name == "H":
                            dense_half(s, *dense)
                            s += 1
                            if rn is None and s == HALVES:
                                ab_turn()
                        elif rn is None:
                            continue
                        elif name in PE_TAIL:
                            if before:
                                tail(name, rn - 1)
                        else:
                            run_stage(name, rn)

                G0 = l * G_LAYER
                head((G0, 0, l * 8), None)
                ab_sums()
                head((G0, 6, l * 8 + 1), l * 8, before=False)
                with pe.Fori(0, 3) as p:
                    for half in range(2):
                        head((G0 + p * 3 + 3, 6 * half, l * 8 + p * 2 + (2 + half)), l * 8 + p * 2 + (1 + half))
                head((G0 + 12, 0, None), l * 8 + 7)

                last = l * 8 + 7
                pe.wait_ge(csq_done, l * 7 + 7)
                for c in range(NC):
                    m = mm(bank[5][:, 8 + c:9 + c], csum[:, c * P:c * P + P], ones[:, 0:1])
                m.then_inc(stat, 1)

                def first_unit(c):
                    if c < 2 * SLOTS:
                        pe.wait_ge(lo_g, G0 * 4 + (48 + c + 1 + SLOTS))
                    else:
                        pe.wait_ge(lo_v, l * (V_LAYER * 4) + (V_T * 4 + c - 2 * SLOTS + 1 + SLOTS))

                for m_ in range(PRE):
                    c = 2 * PRE + m_
                    first_unit(c)
                    for k in range(KT):
                        if m_ == 0 and k == 2:
                            pe.wait_ge(var_done, l * 4 + 3)
                            tail("so", last)
                        if m_ == 0 and k == 4:
                            pe.wait_ge(gate_done, l * (2 * PRE) + 5)
                            pe.wait_ge(fbc_done, l * 4 + 3)
                            for q in range(NC):
                                m = mm(bank[6][:, q * P:q * P + P], fbc[:, q, :], ident)
                            m.then_inc(bc, 1)
                        if m_ == 0 and k == KT - 1:
                            tail("fb", last)
                            pe.wait_ge(ve_tl.sem, ve_tl.after(last, "olo"))
                        m = three(m_, c % SLOTS, k, o_hi, o_lo, k, k == 0, k == KT - 1)
                    m.then_inc(used, 1)
                for m_ in range(PRE):
                    c = 3 * PRE + m_
                    first_unit(c)
                    for k in range(KT):
                        if m_ == 0:
                            pe.wait_ge((clo_g, clo_v)[k % 2], l * 4 + (k // 2 + 1))
                        m = three(3 + m_, c % SLOTS, k, c_hi, c_lo, k, k == 0, k == KT - 1)
                    m.then_inc(used, 1)

                N = KT - PRE
                with pe.Fori(0, N) as i:
                    for c in range(4):
                        pe.wait_ge(lo_v, l * (V_LAYER * 4) + i * 4 + ((V_T + 1) * 4 + c + 1 + SLOTS))
                        pe.wait_ge(t_done, l * (2 * PRE) + 4)
                        if c < 2:
                            pe.wait_ge(th_done, l * (2 * N) + i * 2 + (c + 1))
                        else:
                            pe.wait_ge(ta_done, l * (2 * N) + i * 2 + (c - 2 + 1))
                        for k in range(KT):
                            a_hi, a_lo = ((h_hi, h_lo), (h_hi, h_lo), (o_hi, o_lo), (c_hi, c_lo))[c]
                            m = three(c, c, k, a_hi, a_lo, k, k == 0, k == KT - 1)
                        m.then_inc(used, 1)
                with pe.Fori(0, 2) as i:
                    for j in range(4):
                        pe.wait_ge(lo_v, l * (V_LAYER * 4) + i * 4 + (V_O * 4 + j + 1 + SLOTS))
                        pe.wait_ge(x_upd, l * 24 + i * 4 + (16 + j - 1))
                        for k in range(KT):
                            if j == 0:
                                pe.wait_ge((mglo_g, mglo_v)[k % 2], l * 4 + (k // 2 + 1))
                            m = three(4 + j % 2, j, k, mg_hi, mg_lo, k, k == 0, k == KT - 1)
                        m.then_inc(used, 1)
                ffn(l, 1, R_F2, V_F2, R_D2, V_D2, 2, l * 4 + 3, 24)

            norm_stats(3 * DEPTH)
            for c in range(NC):
                for half in range(2):
                    n = 2 * c + half
                    if n >= 2:
                        pe.wait_ge(fin_y, n - 1)
                    for k in range(4):
                        m = nc.tensor.transpose(bank[n % 2][:, k * P:k * P + P], xT[:, 4 * half + k, c * P:c * P + P], ident)
                    m.then_inc(fin_t, 1)


        @block.scalar
        def _(act):
            def hi(Rd, c):
                act.wait_ge(raw_landed[c % SLOTS], Rd * 16 + 16 * (c // SLOTS + 1))
                act.wait_ge(used, Rd * 4 + (c + 1))
                nc.scalar.activation(w_hi[c % SLOTS][:, :], raw[c % SLOTS][:, :], ACT.Copy).then_inc(hi_done, 1)

            def square_x(rn, m, upd):
                act.wait_ge(x_upd, upd)
                if m >= 3:
                    act.wait_ge(ssq_done, rn * 7 + (m - 2))
                dst = ssq if m == 0 else sqb[m % 2]
                nc.scalar.activation(dst[:, :], xT[:, m, :], ACT.Square).then_inc(sq_done, 1)

            def norm_hi(nh, l):
                for k in range(KT):
                    act.wait_ge(hf_done, l * 8 + (k + 1))
                    nc.scalar.activation(h_hi[:, k, :], hb[k % 4][:, :], ACT.Copy).then_inc(hhi_done, 1)

            def x_hi(k, row):
                nc.scalar.activation(h_hi[:, k, :], xT[:, k, :], ACT.Copy, scale=pcol[:, k, row:row + 1]).then_inc(hhi_done, 1)

            def ffn(l, w, r_f, r_d, nrm_i, upd0):
                with act.Fori(0, FT // 2) as i:
                    Rd = l * R_LAYER + i + r_f
                    for c in range(4):
                        if c % 2 == 0:
                            act.wait_ge(gs_done, l * (2 * FT) + i * 2 + (w * FT + c // 2 + 1 + 2))
                            nc.scalar.activation(sg_f[c // 2][:, :], sg_f[c // 2][:, :], ACT.Silu).then_inc(silu_done, 1)
                        hi(Rd, c + 4)
                for i in range(2):
                    for c in range(12):
                        last = i == 1 and c == 11
                        if not last and not (w == 1 and i == 1 and c >= 8):
                            hi(l * R_LAYER + (r_d + 3 * i), c + 4)
                        if c % 3 == 2:
                            m = 4 * i + c // 3
                            square_x(l * 3 + nrm_i + 1, m, l * 24 + (upd0 + m + 1))
                        if last and w == 0:
                            hi(l * R_LAYER + (r_d + 3 * i), c + 4)

            for m in range(KT):
                act.wait_ge(x_upd, m + 1)
                dst = ssq if m == 0 else x_sq[:, m, :]
                nc.scalar.activation(dst[:, :], xT[:, m, :], ACT.Square).then_inc(sq_done, 1)
            with act.Fori(0, DEPTH) as l:
                hi(l * R_LAYER, 0)
                act.wait_ge(par_norm, l + 1)
                for k in range(KT):
                    x_hi(k, PR_F1)
                for c in range(1, 4):
                    hi(l * R_LAYER, c)
                ffn(l, 0, R_F1, R_D1, 0, 8)
                act.wait_ge(wab_in, l * 64 + 64)
                nc.scalar.activation(wab_hi[:, :, :], wab_raw[:, :, :], ACT.Copy).then_inc(abhi_done, 1)
                norm_hi(l * 3 + 1, l)

                def ab_first():
                    act.wait_ge(ab_v, l * AB_V + 4)
                    nc.scalar.activation(abw[:, 1, :, :], abw[:, 1, :, :], ACT.Exp, scale=-1.0).then_inc(ab_a, 1)
                    nc.scalar.activation(abw[:, 5, :, :].rearrange("p h c -> p c h"), ab[:, :, 8:16], ACT.Tanh, scale=0.5).then_inc(ab_a, 1)
                    nc.scalar.activation(alb[:, 0, :], alb[:, 0, :], ACT.Exp).then_inc(ab_a, 1)

                def ab_exps():
                    act.wait_ge(ab_v, l * AB_V + AB_G + 1)
                    act.wait_ge(ab_pe, l * 3 + 3)
                    nc.scalar.activation(abw[:, 2, :, :], hsc[:, :, HS_GC, :], ACT.Exp).then_inc(ab_a, 1)
                    nc.scalar.activation(hsc[:, :, HS_KD, :], abw[:, 0, :, :], ACT.Exp).then_inc(ab_a, 1)
                    nc.scalar.activation(hsc[:, :, HS_GL, :], abw[:, 3, :, :], ACT.Exp).then_inc(ab_a, 1)

                def dense_steps(t, Rd, c0, rd):
                    act.wait_ge(used, Rd * 4 + (c0 + t + 1 + SLOTS))
                    bk = bank[6 + t % 2]
                    if rd is None:
                        if t == 0:
                            act.wait_ge(ve_dn.sem, ve_dn.after(l * 8 + 7, "vT"))
                            act.wait_ge(pe_dn.sem, pe_dn.after(l * 8 + 7, "vt"))
                        m = t // 2 + PRE * (t % 2)
                        nc.scalar.activation(mg[:, m, :], bk[:, :], ACT.Tanh, scale=0.5).then_inc(gate_done, 1)
                    elif t < 3:
                        n, dst, acc = (("q", q_raw, qa), ("k", k_raw, ka), ("v", v_raw, va))[t]
                        act.wait_ge(ve_ds.sem, ve_ds.after(rd - 1, f"{n}3"))
                        nc.scalar.activation(dst[:, SC - 1:], bk[:, :], ACT.Copy).then_inc(*ac_ds.step(f"{n}_raw"))
                        act.wait_ge(ve_dn.sem, ve_dn.after(rd - 1, f"{n}T"))
                        if n == "v":
                            act.wait_ge(pe_dn.sem, pe_dn.after(rd - 1, "vt"))
                        act.wait_ge(ve_ds.sem, ve_ds.after(rd, "dcol"))
                        w = PR_QKV + 3 * (SC - 1) + t
                        nc.scalar.activation(acc[:, :], bk[:, :], ACT.Copy, scale=dcol[:, w:w + 1]).then_inc(*ac_ds.step(f"{n}_tap"))
                    elif t == 3:
                        act.wait_ge(ve_ds.sem, ve_ds.after(rd - 1, "craw"))
                        nc.scalar.activation(gth[:, :], bk[:, :], ACT.Tanh, scale=0.5).then_inc(*ac_ds.step("g_th"))
                    elif t == 4:
                        act.wait_ge(ve_ds.sem, ve_ds.after(rd - 1, "craw"))
                        nc.scalar.activation(valb[:, :], bk[:, :], ACT.Copy).then_inc(*ac_ds.step("val"))
                    else:
                        act.wait_ge(ve_ds.sem, ve_ds.after(rd, "sg"))
                        nc.scalar.activation(gth[:, :], bk[:, :], ACT.Tanh, scale=0.5).then_inc(*ac_ds.step("gt_th"))

                def c_square(m, last=False):
                    act.wait_ge(taps, l * (8 * TAPS) + (m + 2) * TAPS)
                    if m >= 3:
                        act.wait_ge(csq_done, l * 7 + (m - 2))
                    dst = csum if m == 0 else csq[m % 2]
                    nc.scalar.activation(dst[:, :], c_all[:, m, :], ACT.Square).then_inc(cf_done, 1)

                def head(dense, rn):
                    Rd, c0, rd = dense
                    gates = rd is None

                    def ve(n, r=rn):
                        act.wait_ge(ve_dn.sem, ve_dn.after(r, n))

                    def pe_(n, r=rn):
                        act.wait_ge(pe_dn.sem, pe_dn.after(r, n))

                    if rn is not None:
                        pe_("vn3", rn - 1)
                        act.wait_ge(ve_ds.sem, ve_ds.after(rn, "v3"))
                        nc.scalar.activation(XT[:, :], va[:, :], ACT.Tanh).then_inc(*ac_dn.step("thv"))
                        act.wait_ge(ve_tl.sem, ve_tl.after(rn - 1, "og"))
                        act.wait_ge(ve_ds.sem, ve_ds.after(rn, "sg"))
                        nc.scalar.activation(sgc[:, :], sgn[:, :], ACT.Copy).then_inc(*ac_dn.step("sgc"))
                        act.wait_ge(po_tl.sem, po_tl.after(rn - 1, "sum"))
                        pe_("kt")
                        for c in range(NC):
                            a = nc.scalar.activation(NT[:, c * P:c * P + P], bank[1][:, c * P:c * P + P], ACT.Square, accum_out=ksum[:, c:c + 1])
                        a.then_inc(*ac_dn.step("ksq"))
                        ve("dmin")
                        nc.scalar.activation(dec[:, :], dec[:, :], ACT.Exp).then_inc(*ac_dn.step("decT"))
                        nc.scalar.activation(qd[:, :], bank[0][:, :], ACT.Exp).then_inc(*ac_dn.step("eg"))
                        for c in range(NC):
                            a = nc.scalar.activation(kd[:, c * P:c * P + P], bank[1][:, c * P:c * P + P], ACT.Copy, scale=hs[:, HS_KD, c:c + 1])
                        a.then_inc(*ac_dn.step("kd"))
                    dense_steps(0, *dense)
                    if rn is not None:
                        pe_("x2t")
                        nc.scalar.activation(X[:, :], bank[0][:, :], ACT.Copy).then_inc(*ac_dn.step("X2"))
                        act.wait_ge(po_dn.sem, po_dn.after(rn, "rk"))
                        for c in range(NC):
                            a = nc.scalar.activation(vs[:, c * P:c * P + P], bank[4][:, c * P:c * P + P], ACT.Copy, scale=sm[:, 3, c:c + 1])
                        a.then_inc(*ac_dn.step("vs"))
                    hi(Rd, c0 + 4)
                    if rn is None:
                        ab_first()
                    for t in range(1, 5):
                        if gates:
                            c_square(2 * t - 2)
                            if t < 4:
                                c_square(2 * t - 1)
                        dense_steps(t, *dense)
                        hi(Rd, c0 + t + 4)
                    if rn is not None:
                        pe_(f"y{LEVELS - 1}")
                        nc.scalar.activation(NT[:, :], qT[:, :], ACT.Square, scale=float(np.sqrt(P * EPS))).then_inc(*ac_dn.step("qsq"))
                        if gates:
                            c_square(KT - 1)
                    if not gates:
                        pe_(f"xy{LEVELS - 1}", rd - 1)
                        act.wait_ge(ve_ds.sem, ve_ds.after(rd, "k3"))
                        nc.scalar.activation(Y[:, :], ka[:, :], ACT.Tanh).then_inc(*ac_dn.step("thk"))
                        nc.scalar.activation(X[:, :], qa[:, :], ACT.Tanh).then_inc(*ac_dn.step("thq"))
                    dense_steps(5, *dense)
                    if rn is not None:
                        pe_("os3")
                        nc.scalar.activation(attn[:, :], bank[4][:, :], ACT.Square, scale=float(np.sqrt(1.0 / P))).then_inc(*ac_tl.step("osq"))
                    hi(Rd, c0 + 9)

                Rh = l * R_LAYER + R_H
                head((Rh, 0, l * 8), None)
                ab_exps()
                head((Rh, 6, l * 8 + 1), l * 8)
                with act.Fori(0, 3) as p:
                    for half in range(2):
                        head((Rh + p * 3 + 3, 6 * half, l * 8 + p * 2 + (2 + half)), l * 8 + p * 2 + (1 + half))
                Rt = l * R_LAYER + R_T
                head((Rt, 0, None), l * 8 + 7)

                def c_tanh(k):
                    act.wait_ge(cn_done, l * 8 + (k + 1))
                    if k >= 2:
                        act.wait_ge(cp_done, l * 8 + (k - 1))
                    nc.scalar.activation(cth[k % 2][:, :], hb[k % 4][:, :], ACT.Tanh).then_inc(cth_done, 1)

                c_tanh(0)
                for k in range(KT):
                    if k < KT - 1:
                        c_tanh(k + 1)
                    act.wait_ge(cp_done, l * 8 + (k + 1))
                    nc.scalar.activation(c_hi[:, k, :], hb[k % 4][:, :], ACT.Copy).then_inc(chi_done, 1)
                    if k in (3, 6):
                        hi(Rt, (10, 11)[k // 4])
                for c in range(12, 16):
                    hi(Rt, c)
                N = KT - PRE

                def mg_round(k):
                    act.wait_ge(mg_done, l * 8 + (k + 2))
                    nc.scalar.activation(mg_hi[:, k, :], mg[:, k, :], ACT.Copy).then_inc(mghi_done, 1)

                def gates(m, last=False):
                    Rd = l * R_LAYER + m + (R_T + 3)
                    for c in range(4):
                        if last and c == 3:
                            act.wait_ge(used, Rd * 4 + (2 + 1 + SLOTS))
                            for k in range(KT - 1):
                                mg_round(k)
                        if c < 2:
                            act.wait_ge(used, Rd * 4 + (c + 1 + SLOTS))
                            act.wait_ge(clo_g, l * 4 + 4)
                            act.wait_ge(ta_done, l * (2 * N) + m * 2 + (c + 1))
                            nc.scalar.activation((thA, thB)[c][:, :], bank[c][:, :], ACT.Tanh, scale=0.5).then_inc(th_done, 1)
                        hi(Rd, c + 4)

                with act.Fori(0, N - 1) as m:
                    gates(m)
                gates(N - 1, last=True)
                mg_round(KT - 1)
                for i in range(2):
                    for c in range(4):
                        hi(l * R_LAYER + (R_O + i), c + 4)
                        square_x(l * 3 + 2, 4 * i + c, l * 24 + (16 + 4 * i + c + 1))
                        x_hi(4 * i + c, PR_F2)
                ffn(l, 1, R_F2, R_D2, 2, 24)

        @block.vector
        def _(dve):
            tt, ts, stt = nc.vector.tensor_tensor, nc.vector.tensor_scalar, nc.vector.scalar_tensor_tensor

            def lo(Rd, Vd, c):
                dve.wait_ge(hi_done, Rd * 4 + (c + 1))
                tt(w_lo[c % SLOTS][:, :], raw[c % SLOTS][:, :], w_hi[c % SLOTS][:, :].bitcast(F32), ALU.subtract).then_inc(lo_v, 1)

            def norm_factor(rn, nf):
                dve.wait_ge(stat, nf + 1)
                ts(nrm[:, 0, :], bank[6][:, 0:NC], 1.0 / D, EPS, ALU.mult, ALU.add).then_inc(var_done, 1)

            def norm_fbc(nf):
                dve.wait_ge(rs_done, nf + 1)
                nc.vector.tensor_copy(fbc[:, :, :], spread(nrm[:, 1, :])).then_inc(fbc_done, 1)

            def norm_h(nh, nf, row, l):
                norm_factor(nh, nf)
                norm_fbc(nf)
                dve.wait_ge(bc, nf + 1)
                for k in range(KT + 1):
                    if k < KT:
                        if k >= 4:
                            dve.wait_ge((hlo_g, hlo_v)[k % 2], l * 4 + ((k - 4) // 2 + 1))
                        stt(out=hb[k % 4][:, :], in0=xT[:, k, :], scalar=pcol[:, k, row:row + 1], in1=bank[7][:, :],
                            op0=ALU.mult, op1=ALU.mult).then_inc(hf_done, 1)
                    if k and k % 2 == 0:
                        dve.wait_ge(hhi_done, nh * 8 + k)
                        tt(h_lo[:, k - 1, :], hb[(k - 1) % 4][:, :], h_hi[:, k - 1, :].bitcast(F32), ALU.subtract).then_inc(hlo_v, 1)

            def add_x(m, Rd, c, upd, scale, bk):
                dve.wait_ge(used, Rd * 4 + (c + 1 + SLOTS))
                stt(out=xT[:, m, :], in0=bank[bk][:, :], scalar=scale, in1=xT[:, m, :], op0=ALU.mult, op1=ALU.add).then_inc(x_upd, 1)

            def x_rest(k, row, nh):
                dve.wait_ge(hhi_done, nh * 8 + (k + 1))
                stt(out=h_lo[:, k, :], in0=xT[:, k, :], scalar=pcol[:, k, row:row + 1], in1=h_hi[:, k, :].bitcast(F32),
                    op0=ALU.mult, op1=ALU.subtract).then_inc(hx_done, 1)

            def ffn(l, w, r_f, v_f, r_d, v_d, nrm_i, nf, row):
                norm_factor(None, nf)
                norm_fbc(nf)
                dve.wait_ge(bc, nf + 1)
                nc.vector.tensor_copy(ssq[:, :], bank[7][:, :]).then_inc(rinv_done, 1)
                with dve.Fori(0, FT // 2) as i:
                    Rd, Vd = l * R_LAYER + i + r_f, l * V_LAYER + i + v_f
                    for c in range(4):
                        f = c // 2
                        n = l * (2 * FT) + i * 2 + (w * FT + f)
                        dve.wait_ge(used, Rd * 4 + (c + 1 + SLOTS))
                        if c % 2 == 0:
                            dve.wait_ge(rinv_done, l * 2 + (w + 1))
                            tt(sg_f[f][:, :], bank[c][:, :], ssq[:, :], ALU.mult).then_inc(gs_done, 1)
                        else:
                            tt(a_f[f][:, :], bank[c][:, :], ssq[:, :], ALU.mult).then_inc(ub_done, 1)
                            dve.wait_ge(ub_done, n + (1 + 2))
                            dve.wait_ge(silu_done, n + 1)
                            tt(a_f[f][:, :], sg_f[f][:, :], a_f[f][:, :], ALU.mult).then_inc(prod_done, 1)
                            dve.wait_ge(prod_done, n + 1)
                            ts(act_hi[:, i * 2 + f, :], a_f[f][:, :], 1.0, None, ALU.mult).then_inc(acthi_done, 1)
                            dve.wait_ge(acthi_done, n + 1)
                            tt(act_lo[:, i * 2 + f, :], a_f[f][:, :], act_hi[:, i * 2 + f, :].bitcast(F32), ALU.subtract).then_inc(actlo_done, 1)
                        lo(Rd, Vd, c + 4)
                for i in range(2):
                    for c in range(12):
                        if not (i == 1 and c >= 8):
                            lo(l * R_LAYER + (r_d + 3 * i), None, c + 4)
                        if c % 3 == 2:
                            add_x(4 * i + c // 3, l * R_LAYER + (r_d + 3 * i), c, None, 0.5, 4 + (c // 3) % 2)

            nc.vector.memset(ones[:, :], 1.0).then_inc(init, 1)
            nc.vector.memset(pw[:, 0, :], -0.5).then_inc(init, 1)
            nc.vector.memset(pw[:, 1, :], 0.5).then_inc(init, 1)
            nc.vector.memset(prow[:, :], 0.0).then_inc(init, 1)
            dve.wait_ge(xt_done, NC)
            for k in range(KT):
                nc.vector.tensor_copy(xT[:, k, :], bank[k][:, :]).then_inc(x_upd, 1)

            with dve.Fori(0, DEPTH) as l:
                dve.wait_ge(par_t, l + 2)
                for a, b, f in ((PR_F1, PR_QKV, 1.0), (PR_DW, PR_B, 0.5), (PR_B, PR_CN, 1.0), (PR_CN, PR_F1, 0.5), (PR_QKV, PR_N, 0.5)):
                    if a == PR_DW:
                        last.then_inc(par_norm, 1)
                    for half in range(2):
                        pv = bank[half][:, :].rearrange("p (k r) -> p k r", k=4)
                        last = ts(pcol[:, 4 * half:4 * half + 4, a:b], pv[:, :, a:b], f, None, ALU.mult)
                last.then_inc(par_done, 1)
                lo(l * R_LAYER, None, 0)
                dve.wait_ge(par_done, l + 1)
                for k in range(KT):
                    x_rest(k, PR_F1, l * 3)
                for c in range(1, 4):
                    lo(l * R_LAYER, None, c)
                ffn(l, 0, R_F1, V_F1, R_D1, V_D1, 0, l * 4, PR_F1)

                dve.wait_ge(abhi_done, l + 1)
                tt(wab_lo[:, :, :], wab_raw[:, :, :], wab_hi[:, :, :].bitcast(F32), ALU.subtract).then_inc(ablo_done, 1)
                for r in (q_raw, k_raw, v_raw):
                    nc.vector.memset(r[:, 0:SC - 1], 0.0)
                nc.vector.memset(c_raw[:, 0:TAPS - 1], 0.0).then_inc(init, 1)
                norm_h(l * 3 + 1, l * 4 + 1, PR_MIX, l)
                n = [0]

                def ab_step(ins):
                    n[0] += 1
                    ins.then_inc(ab_v, 1)
                    dve.wait_ge(ab_v, l * AB_V + n[0])

                def columns(rd, hd):
                    dve.wait_ge(ve_ds.sem, ve_ds.after(rd - 1, "craw"))
                    dve.wait_ge(ac_ds.sem, ac_ds.after(rd - 1, "v_tap"))
                    ts(dcol[:, :], pcol[:, hd, :], 1.0, None, ALU.mult).then_inc(*ve_ds.step("dcol"))
                    dve.wait_ge(ve_ds.sem, ve_ds.after(rd, "dcol"))

                columns(l * 8, 0)
                dve.wait_ge(ab_pe, l * 3 + 1)
                ab_step(nc.vector.tensor_copy(abT[0:16, :], bank[0][0:16, :]))
                dve.wait_ge(ab_pe, l * 3 + 2)
                ab_step(nc.vector.tensor_copy(ab[:, :, :], bank[1][:, 0:NC * 16].rearrange("p (c o) -> p c o", c=NC)))
                dtb = alb[:, 1, :].rearrange("p (h o) -> p h o", o=1).broadcast_to([P, HEADS, NC])
                z, e, sv, s2, po = (abw[:, i, :, :] for i in (0, 1, 2, 3, 4))
                ab_step(tt(z, ab[:, :, 0:8].rearrange("p c h -> p h c"), dtb, ALU.add))
                ab_step(stt(out=e, in0=z, scalar=-1.0, in1=z, op0=ALU.mult, op1=ALU.max))
                dve.wait_ge(ab_a, l * 6 + 3)
                ab_step(ts(sv, e, 2.0, None, ALU.add))
                nc.vector.reciprocal(sv, sv).then_inc(ab_v, 1)
                n[0] += 1
                dve.wait_ge(ab_v, l * AB_V + n[0])
                ab_step(tt(sv, sv, e, ALU.mult))
                ab_step(tt(s2, sv, sv, ALU.mult))
                ts(po, s2, 1.0 / 17, 1.0 / 15, ALU.mult, ALU.add).then_inc(ab_h, 1)
                hcount = 1
                for q in (13, 11, 9, 7, 5, 3, 1):
                    dve.wait_ge(ab_h, l * 17 + hcount)
                    tt(po, po, s2, ALU.mult).then_inc(ab_h, 1)
                    dve.wait_ge(ab_h, l * 17 + hcount + 1)
                    ts(po, po, 1.0 / q, None, ALU.add).then_inc(ab_h, 1)
                    hcount += 2
                dve.wait_ge(ab_h, l * 17 + hcount)
                tt(po, po, sv, ALU.mult).then_inc(ab_h, 1)
                dve.wait_ge(ab_h, l * 17 + hcount + 1)
                ab_step(ts(z, z, 0.0, None, ALU.max))
                ab_step(stt(out=z, in0=po, scalar=2.0, in1=z, op0=ALU.mult, op1=ALU.add))
                ea = alb[:, 0, :].rearrange("p (h o) -> p h o", o=1).broadcast_to([P, HEADS, NC])
                ab_step(tt(z, z, ea, ALU.mult))
                ab_step(ts(hsc[:, :, HS_BETA, :], abw[:, 5, :, :], 0.5, 0.5, ALU.mult, ALU.add))
                ab_step(ts(hsc[:, :, HS_G, :], z, -1.0, None, ALU.mult))
                assert n[0] == AB_G and hcount == 15

                def ab_sums():
                    dve.wait_ge(ab_pe, l * 3 + 3)
                    sums = bank[1][:, 0:64].rearrange("p (s h c) -> p s h c", s=2, h=HEADS)
                    nc.vector.tensor_copy(hsc[:, :, HS_GC, :], sums[:, 0])
                    nc.vector.tensor_copy(abw[:, 3, :, :], sums[:, 1]).then_inc(ab_h, 1)
                    dve.wait_ge(ab_h, l * 17 + 17)
                    tt(abw[:, 0, :, :], abw[:, 3, :, :], hsc[:, :, HS_GC, :], ALU.subtract).then_inc(ab_v, 1)
                    dve.wait_ge(ab_a, l * 6 + 6)
                    ts(hsc[:, :, HS_NEG, :], abw[:, 2, :, :], -1.0, None, ALU.mult).then_inc(ab_v, 1)

                def head(dense, hn, rn, before=True):
                    dn = rn is not None
                    tap = [0]

                    def fill(k=1):
                        if not dn:
                            return
                        for _ in range(k):
                            j = tap[0]
                            if j == TAPS:
                                return
                            tap[0] += 1
                            src = c_raw[:, j:j + SEQ]
                            if j == 0:
                                dve.wait_ge(ve_ds.sem, ve_ds.after(rn, "craw"))
                                ts(cacc[:, :], src, ncol[:, 0:1], ncol[:, PR_B:PR_B + 1], ALU.mult, ALU.add).then_inc(taps, 1)
                            else:
                                dve.wait_ge(taps, rn * TAPS + (TAPS + j))
                                dst = cacc[:, :] if j < TAPS - 1 else c_all[:, hn, :]
                                stt(out=dst, in0=src, scalar=ncol[:, j:j + 1], in1=cacc[:, :], op0=ALU.mult, op1=ALU.add).then_inc(taps, 1)

                    def ac(n, r=rn):
                        dve.wait_ge(ac_dn.sem, ac_dn.after(r, n))

                    def pe_(n, r=rn):
                        dve.wait_ge(pe_dn.sem, pe_dn.after(r, n))

                    def po_(n, r=rn):
                        dve.wait_ge(po_dn.sem, po_dn.after(r, n))

                    def me(n, r=rn):
                        dve.wait_ge(ve_dn.sem, ve_dn.after(r, n))

                    def conv(t, j):
                        if not dense:
                            fill()
                            return
                        rd = dense[0]
                        n, src, acc = (("q", q_raw, qa), ("k", k_raw, ka), ("v", v_raw, va))[t]
                        if j == 0:
                            dve.wait_ge(ac_ds.sem, ac_ds.after(rd, f"{n}_tap"))
                        else:
                            dve.wait_ge(ve_ds.sem, ve_ds.after(rd, f"{n}{j}"))
                        w = PR_QKV + 3 * j + t
                        stt(out=acc[:, :], in0=src[:, j:j + SEQ], scalar=dcol[:, w:w + 1], in1=acc[:, :],
                            op0=ALU.mult, op1=ALU.add).then_inc(*ve_ds.step(f"{n}{j + 1}"))

                    def silu_gate():
                        if not dense:
                            fill()
                            return
                        rd = dense[0]
                        dve.wait_ge(ac_ds.sem, ac_ds.after(rd, "g_th"))
                        dve.wait_ge(ac_dn.sem, ac_dn.after(rd - 1, "sgc"))
                        stt(out=sgn[:, :], in0=gth[:, :], scalar=1.0, in1=bank[7][:, :], op0=ALU.add, op1=ALU.mult).then_inc(*ve_ds.step("sg"))

                    between = [(("t", "t", "t"), ((0, 0), "t", (0, 1))), (("t", (0, 2), "t"), ("t", "t")),
                               (((1, 0), "t"), ((1, 1), "t", (1, 2))), (("t", "t"), ((2, 0), "t", (2, 1))),
                               (("t", (2, 2), "t"), ("t", "t", "t")), (("t", "t"), ("g",))]

                    def put(items):
                        for x in items:
                            if x == "t":
                                fill()
                            elif x == "g":
                                silu_gate()
                            else:
                                conv(*x)

                    def level(lv):
                        if dn:
                            pe_(f"y{lv}")
                            tt(chunked(Y), chunked(bank[1]), each_chunk(I_LV + lv), ALU.mult).then_inc(*ve_dn.step(f"y{lv}"))
                        put(between[lv][0])
                        if dn:
                            pe_(f"xy{lv}")
                            t = X if lv < LEVELS - 1 else XT
                            tt(t[:, :], t[:, :], bank[2][:, :], ALU.subtract).then_inc(*ve_dn.step(f"x{lv}"))
                            if lv < LEVELS - 1:
                                pe_(f"xt{lv}")
                                tt(XT[:, :], XT[:, :], bank[3][:, :], ALU.subtract).then_inc(*ve_dn.step(f"xt{lv}"))
                        put(between[lv][1])

                    if dn:
                        dve.wait_ge(taps, rn * TAPS + TAPS)
                        me("vn3", rn - 1)
                        dve.wait_ge(ab_v, (l + 1) * AB_V)
                        ts(ncol[:, :], pcol[:, hn, :], 1.0, None, ALU.mult)
                        ts(hs[:, :, :], hsc[:, hn, :, :], 1.0, None, ALU.mult).then_inc(*ve_dn.step("hs"))
                        me("hs")
                        nc.vector.tensor_copy(chunked(dec), spread(hs[:, HS_G, :])).then_inc(*ve_dn.step("gbc"))

                        def act_of(n, src, dst, th):
                            ac(f"th{n}")
                            stt(out=dst[:, :], in0=th[:, :], scalar=1.0, in1=src[:, :], op0=ALU.add, op1=ALU.mult).then_inc(*ve_dn.step(f"{n}T"))

                        act_of("k", ka, kT, Y)
                        if before:
                            tail("og", rn - 1)
                        act_of("q", qa, qT, X)
                        act_of("v", va, va, XT)
                        pe_("gr")
                        for c in range(NC):
                            a = ts(dec[:, c * P:c * P + P], bank[0][:, c * P:c * P + P], hs[:, HS_GC, c:c + 1], 0.0, ALU.subtract, ALU.min)
                        a.then_inc(*ve_dn.step("dmin"))
                        if before:
                            tail("vE", rn - 1)
                        ac("ksq")
                        ts(sm[:, 0, :], ksum[:, :], EPS, None, ALU.add).then_inc(*ve_dn.step("skE"))
                        me("skE")
                        nc.vector.reciprocal(sm[:, 1, :], sm[:, 0, :]).then_inc(*ve_dn.step("rden"))
                        me("rden")
                        tt(sm[:, 2, :], sm[:, 1, :], hs[:, HS_BETA, :], ALU.mult).then_inc(*ve_dn.step("bnk2"))
                        dve.wait_ge(ac_ds.sem, ac_ds.after(rn, "gt_th"))
                        dve.wait_ge(taps, rn * TAPS + TAPS)
                        stt(out=c_raw[:, TAPS - 1:], in0=gth[:, :], scalar=1.0, in1=valb[:, :], op0=ALU.add, op1=ALU.mult).then_inc(*ve_ds.step("craw"))
                        if before:
                            tail("fbc", rn - 1)
                    if dense and dn:
                        columns(*dense)
                    if dn:
                        me("bnk2")
                        po_("decs")
                        pe_("kk")
                        for c in range(NC):
                            t = slice(c * P, c * P + P)
                            a = stt(out=NT[:, t], in0=bank[2][:, t], scalar=sm[:, 2, c:c + 1], in1=decs[:, t], op0=ALU.mult, op1=ALU.mult)
                        a.then_inc(*ve_dn.step("NT"))
                        if before:
                            tail("oF", rn - 1, hn - 1)
                        me("NT")
                        tt(chunked(XT), chunked(NT), each_chunk(I_M1T), ALU.mult).then_inc(*ve_dn.step("m1"))
                        if before:
                            tail("ohi", rn - 1, hn - 1)
                        else:
                            fill()
                        me("m1")
                        tt(chunked(XT), each_chunk(I_ID), chunked(XT), ALU.subtract).then_inc(*ve_dn.step("x2T"))
                        if before:
                            tail("olo", rn - 1, hn - 1)
                        pe_("kq")
                        po_("deci")
                        tt(attn[:, :], attn[:, :], bank[3][:, :], ALU.mult).then_inc(*ve_dn.step("attnT"))
                        fill(3)
                    for lv in range(LEVELS):
                        level(lv)
                    if dn:
                        for c in range(NC):
                            t = slice(c * P, c * P + P)
                            if c:
                                pe_(f"p{c}")
                                stt(out=R[:, :], in0=bank[0][:, 0:P], scalar=hs[:, HS_NEG, c:c + 1], in1=vs[:, t],
                                    op0=ALU.mult, op1=ALU.add).then_inc(*ve_dn.step(f"r{c}"))
                            pe_(f"vn{c}")
                            ts(VN[:, :], bank[1][:, 0:P], sm[:, 2, c:c + 1], None, ALU.mult).then_inc(*ve_dn.step(f"vn{c}"))
                            fill()
                            if c < NC - 1:
                                pe_(f"os{c}")
                                if c == 0:
                                    ts(S[:, :], bank[2][:, 0:P], 1.0, None, ALU.mult).then_inc(*ve_dn.step("s0"))
                                else:
                                    me(f"s{c - 1}")
                                    stt(out=S[:, :], in0=S[:, :], scalar=hs[:, HS_GL, c:c + 1], in1=bank[2][:, 0:P],
                                        op0=ALU.mult, op1=ALU.add).then_inc(*ve_dn.step(f"s{c}"))
                                fill()
                        fill(TAPS)

                def tail(name, rn, hn=None):
                    if name == "og":
                        dve.wait_ge(ac_tl.sem, ac_tl.after(rn, "osq"))
                        a = stt(out=og[:, :], in0=bank[4][:, :], scalar=hnh[:, 0:1], in1=sgc[:, :], op0=ALU.mult, op1=ALU.mult)
                    elif name == "vE":
                        dve.wait_ge(pe_tl.sem, pe_tl.after(rn, "so"))
                        a = ts(sm[:, 4, :], bank[5][:, 0:NC], P * EPS * EPS, None, ALU.add)
                    elif name == "fbc":
                        dve.wait_ge(po_tl.sem, po_tl.after(rn, "rs"))
                        a = nc.vector.tensor_copy(fbc[:, :, :], spread(sm[:, 5, :]))
                    elif name == "oF":
                        dve.wait_ge(pe_tl.sem, pe_tl.after(rn, "fb"))
                        a = tt(og[:, :], og[:, :], bank[5][:, :], ALU.mult)
                    elif name == "ohi":
                        dve.wait_ge(ve_tl.sem, ve_tl.after(rn, "oF"))
                        a = ts(o_hi[:, hn, :], og[:, :], 1.0, None, ALU.mult)
                    else:
                        dve.wait_ge(ve_tl.sem, ve_tl.after(rn, "ohi"))
                        a = tt(o_lo[:, hn, :], og[:, :], o_hi[:, hn, :].bitcast(F32), ALU.subtract)
                    a.then_inc(*ve_tl.step(name))

                dve.wait_ge(wab_in, l * 64 + 64)
                ts(hnh[:, :], hnw[:, :], 0.5, None, ALU.mult).then_inc(hn_done, 1)
                dve.wait_ge(hn_done, l + 1)
                head((l * 8, 0), None, None)
                ab_sums()
                dve.wait_ge(const_in, 16)
                head((l * 8 + 1, 1), 0, l * 8, before=False)
                with dve.Fori(0, 3) as p:
                    for half in range(2):
                        head((l * 8 + p * 2 + (2 + half), p * 2 + (2 + half)), p * 2 + (1 + half), l * 8 + p * 2 + (1 + half))
                head(None, 7, l * 8 + 7)

                last, Rt = l * 8 + 7, l * R_LAYER + R_T

                def c_norm(k):
                    if k >= 4:
                        dve.wait_ge((clo_g, clo_v)[k % 2], l * 4 + ((k - 4) // 2 + 1))
                    stt(out=hb[k % 4][:, :], in0=c_all[:, k, :], scalar=pcol[:, k, PR_CN:PR_CN + 1], in1=bank[6][:, :],
                        op0=ALU.mult, op1=ALU.mult).then_inc(cn_done, 1)

                def c_silu(k):
                    dve.wait_ge(cth_done, l * 8 + (k + 1))
                    stt(out=hb[k % 4][:, :], in0=cth[k % 2][:, :], scalar=1.0, in1=hb[k % 4][:, :], op0=ALU.add, op1=ALU.mult).then_inc(cp_done, 1)

                def c_rest(k):
                    dve.wait_ge(chi_done, l * 8 + (k + 1))
                    tt(c_lo[:, k, :], hb[k % 4][:, :], c_hi[:, k, :].bitcast(F32), ALU.subtract).then_inc(clo_v, 1)

                def gated(n):
                    dve.wait_ge(used, Rt * 4 + (2 * PRE + n + 1 + SLOTS))
                    dve.wait_ge(gate_done, (l + 1) * (2 * PRE))
                    stt(out=mg[:, n, :], in0=mg[:, n, :], scalar=1.0, in1=bank[n][:, :], op0=ALU.add, op1=ALU.mult).then_inc(t_done, 1)

                dve.wait_ge(stat, l * 4 + 3)
                ts(nrm[:, 0, :], bank[5][:, 8:8 + NC], 1.0 / D, EPS, ALU.mult, ALU.add).then_inc(var_done, 1)
                tail("og", last)
                norm_fbc(l * 4 + 2)
                lo(Rt, None, 8)
                tail("vE", last)
                lo(Rt, None, 9)
                dve.wait_ge(bc, l * 4 + 3)
                tail("fbc", last)
                tail("oF", last)
                tail("ohi", last, 7)
                tail("olo", last, 7)
                dve.wait_ge(bc, l * 4 + 3)
                c_norm(0)
                c_norm(1)
                for k in range(KT):
                    if k + 2 < KT:
                        c_norm(k + 2)
                    c_silu(k)
                    if k % 2 == 0 and k:
                        c_rest(k - 1)
                    if k == 4:
                        gated(0)
                    if k in (5, 7):
                        lo(Rt, None, 10 + k // 7)
                c_rest(KT - 1)
                for n in range(1, 2 * PRE):
                    gated(n)
                    if n >= 2:
                        lo(Rt, None, 10 + n)
                    if n >= PRE:
                        dve.wait_ge(t_done, l * (2 * PRE) + (n + 1))
                        tt(mg[:, n - PRE, :], mg[:, n - PRE, :], mg[:, n, :], ALU.add).then_inc(mg_done, 1)

                N = KT - PRE

                def mg_rest(k):
                    dve.wait_ge(mghi_done, l * 8 + (k + 1))
                    tt(mg_lo[:, k, :], mg[:, k, :], mg_hi[:, k, :].bitcast(F32), ALU.subtract).then_inc(mglo_v, 1)

                def gates(m, last=False):
                    Rd = l * R_LAYER + m + (R_T + 3)
                    n = l * (2 * N) + m * 2
                    for c in range(4):
                        if last and c == 3:
                            for k in range(1, KT - 1, 2):
                                mg_rest(k)
                        if c >= 2:
                            dve.wait_ge(used, Rd * 4 + (c + 1 + SLOTS))
                            dve.wait_ge(mg_done, l * 8 + m + (PRE + 1))
                            dve.wait_ge(th_done, n + (c - 2 + 1 + 2))
                            stt(out=(t0, t1)[c - 2][:, :], in0=(thA, thB)[c - 2][:, :], scalar=1.0, in1=bank[c][:, :],
                                op0=ALU.add, op1=ALU.mult).then_inc(ta_done, 1)
                        if c == 3:
                            dve.wait_ge(ta_done, n + 4)
                            tt(mg[:, m + PRE, :], t0[:, :], t1[:, :], ALU.add).then_inc(mg_done, 1)
                        lo(Rd, None, c + 4)

                with dve.Fori(0, N - 1) as m:
                    gates(m)
                gates(N - 1, last=True)
                mg_rest(KT - 1)
                for i in range(2):
                    for c in range(4):
                        lo(l * R_LAYER + (R_O + i), None, c + 4)
                        add_x(4 * i + c, l * R_LAYER + (R_O + i), c, None, 0.5, 4 + c % 2)
                        x_rest(4 * i + c, PR_F2, l * 3 + 2)
                ffn(l, 1, R_F2, V_F2, R_D2, V_D2, 2, l * 4 + 3, PR_F2)

            norm_factor(None, 4 * DEPTH)
            dve.wait_ge(rs_done, 4 * DEPTH + 1)
            dve.wait_ge(par_in, DEPTH * 160 + 16)
            for c in range(NC):
                for half in range(2):
                    n = 2 * c + half
                    dve.wait_ge(fin_t, n + 1)
                    cols = slice(half * 512, half * 512 + 512)
                    stt(out=raw[c][:, cols], in0=bank[n % 2][:, :], scalar=nrm[:, 1, c:c + 1], in1=prow[:, cols],
                        op0=ALU.mult, op1=ALU.mult).then_inc(fin_y, 1)

        @block.gpsimd
        def _(pool):
            tt = nc.gpsimd.tensor_tensor
            for s_, n_ in ((lo_v, SLOTS), (lo_g, SLOTS), (used, SLOTS), (gs_done, 2), (ub_done, 2), (th_done, 2), (ta_done, 2),
                           (par_t, 1), (taps, TAPS), (mg_done, 1)):
                pool.sem_inc(s_, n_)
            for st in (pe_dn, ve_dn, ac_dn, po_dn, pe_tl, ve_tl, ac_tl, po_tl, ac_ds, ve_ds):
                pool.sem_inc(st.sem, len(st.names))

            def lo(Rd, c):
                pool.wait_ge(hi_done, Rd * 4 + (c + 1))
                tt(w_lo[c % SLOTS][:, :], raw[c % SLOTS][:, :], w_hi[c % SLOTS][:, :].bitcast(F32), ALU.subtract).then_inc(lo_g, 1)

            def sum_squares(done, sums, n, base):
                for m in range(1, n + 1):
                    pool.wait_ge(done, base * 8 + (m + 1))
                    if m > 1:
                        pool.wait_ge(sums, base * n + (m - 1))
                    tt(ssq[:, :], ssq[:, :], sqb[m % 2][:, :], ALU.add).then_inc(sums, 1)

            def inverse_root(nf):
                pool.wait_ge(var_done, nf + 1)
                tt(nrm[:, 1, :], nrm[:, 0, :], pw[:, 0, :], ALU.pow).then_inc(rs_done, 1)

            def h_rest(nh, l):
                for k in range(0, KT, 2):
                    pool.wait_ge(hhi_done, nh * 8 + (k + 1))
                    tt(h_lo[:, k, :], hb[k % 4][:, :], h_hi[:, k, :].bitcast(F32), ALU.subtract).then_inc(hlo_g, 1)

            pool.wait_ge(init, 4)
            for m in range(1, KT):
                pool.wait_ge(sq_done, m + 1)
                if m > 1:
                    pool.wait_ge(ssq_done, m - 1)
                tt(ssq[:, :], ssq[:, :], x_sq[:, m, :], ALU.add).then_inc(ssq_done, 1)
            with pool.Fori(0, DEPTH) as l:
                inverse_root(l * 4)
                sum_squares(sq_done, ssq_done, KT - 1, l * 3 + 1)
                Rh = l * R_LAYER + R_H
                inverse_root(l * 4 + 1)
                h_rest(l * 3 + 1, l)
                for c in range(SLOTS):
                    lo(Rh, c)

                def c_sum(m):
                    pool.wait_ge(cf_done, l * 8 + (m + 1))
                    if m > 1:
                        pool.wait_ge(csq_done, l * 7 + (m - 1))
                    tt(csum[:, :], csum[:, :], csq[m % 2][:, :], ALU.add).then_inc(csq_done, 1)

                def head(Rd, c0, rn, before=True, gates=False):
                    def ac(n):
                        pool.wait_ge(ac_dn.sem, ac_dn.after(rn, n))

                    def ve(n):
                        pool.wait_ge(ve_dn.sem, ve_dn.after(rn, n))

                    if rn is not None:
                        if before:
                            square_sum(rn - 1)
                            mean_root(rn - 1)
                        ac("decT")
                        tt(chunked(decs), chunked(dec), each_chunk(I_STRICT), ALU.mult).then_inc(*po_dn.step("decs"))
                        tt(chunked(attn), chunked(dec), each_chunk(I_INCL), ALU.mult).then_inc(*po_dn.step("deci"))
                        ve("skE")
                        tt(sm[:, 3, :], sm[:, 0, :], pw[:, 1, :], ALU.pow).then_inc(*po_dn.step("rk"))
                        lo(Rd, c0 + 3)
                        ac("eg")
                        ve("qT")
                        tt(qd[:, :], qd[:, :], qT[:, :], ALU.mult).then_inc(*po_dn.step("qd"))
                    for t in range(4):
                        lo(Rd, c0 + t + 4)
                        if gates:
                            for m in ((1,), (2, 3), (4, 5), (6,))[t]:
                                c_sum(m)

                def square_sum(rn):
                    pool.wait_ge(ac_dn.sem, ac_dn.after(rn, "qsq"))
                    pool.wait_ge(ac_tl.sem, ac_tl.after(rn, "osq"))
                    tt(attn[:, :], attn[:, :], NT[:, :], ALU.add).then_inc(*po_tl.step("sum"))

                def mean_root(rn):
                    pool.wait_ge(ve_tl.sem, ve_tl.after(rn, "vE"))
                    tt(sm[:, 5, :], sm[:, 4, :], pw[:, 0, :], ALU.pow).then_inc(*po_tl.step("rs"))

                head(Rh, 0, None)
                lo(Rh, 8)
                head(Rh, 6, l * 8, before=False)
                lo(Rh, 14)
                with pool.Fori(0, 3) as p:
                    for half in range(2):
                        head(Rh + p * 3 + 3, 6 * half, l * 8 + p * 2 + (1 + half))
                        lo(Rh + p * 3 + 3, 6 * half + 8)
                Rt = l * R_LAYER + R_T
                head(Rt, 0, l * 8 + 7, gates=True)
                c_sum(KT - 1)
                square_sum(l * 8 + 7)
                inverse_root(l * 4 + 2)
                mean_root(l * 8 + 7)
                for k in range(0, KT, 2):
                    pool.wait_ge(chi_done, l * 8 + (k + 1))
                    tt(c_lo[:, k, :], hb[k % 4][:, :], c_hi[:, k, :].bitcast(F32), ALU.subtract).then_inc(clo_g, 1)
                for k in range(0, KT, 2):
                    pool.wait_ge(mghi_done, l * 8 + (k + 1))
                    tt(mg_lo[:, k, :], mg[:, k, :], mg_hi[:, k, :].bitcast(F32), ALU.subtract).then_inc(mglo_g, 1)
                sum_squares(sq_done, ssq_done, KT - 1, l * 3 + 2)
                inverse_root(l * 4 + 3)
                sum_squares(sq_done, ssq_done, KT - 1, l * 3 + 3)
            inverse_root(4 * DEPTH)


_INS = ["x", "ffn1_norm", "ffn1_w_gate", "ffn1_w_up", "ffn1_w_down", "mix_norm", "w_in", "qkv_conv_w", "a_log",
        "dt_bias", "head_norm", "w_a_out", "dw_conv_w", "dw_conv_b", "conv_norm", "w_b_out", "w_o", "ffn2_norm",
        "ffn2_w_gate", "ffn2_w_up", "ffn2_w_down", "final_norm"]


def kernel(**inputs):
    import concourse.bacc as _bacc
    from concourse.bass_utils import run_bass_kernel_spmd as _run

    nc = _bacc.Bacc("TRN2", target_bir_lowering=False, num_devices=1)
    arrays, args = {}, []
    for name in _INS + ["consts"]:
        a = constants() if name == "consts" else np.ascontiguousarray(inputs[name])
        arrays[f"in_{name}"] = a
        args.append(nc.dram_tensor(f"in_{name}", a.shape, mybir.dt.from_np(a.dtype), kind="ExternalInput").ap())
    out = nc.dram_tensor("out_x", (1, SEQ, D), F32, kind="ExternalOutput").ap()
    trunk(nc, *args, out)
    return _run(nc, [arrays], core_ids=[0]).results[0]["out_x"]
```
